# Optimizing a Trainium2 kernel written in Bass

```python
import math
import jax, jax.numpy as jnp
from jax import lax
import numpy as np

D_MODEL = 1024
BATCH = 1
SEQ = 256
DEPTH = 2

CTX_LEN = 256
GRID_W = 64

ATTN_WIDTH = D_MODEL // 2
RWKV_WIDTH = D_MODEL - ATTN_WIDTH
ATTN_QK_DIM = 64
ATTN_V_DIM = 2 * ATTN_QK_DIM
ATTN_HEADS = ATTN_WIDTH // ATTN_V_DIM
ROPE_THETA = 10000.0
Q_BLOCK = 128
SUBLN_EPS = 1e-5
RWKV_HEAD = 64
RWKV_HEADS = RWKV_WIDTH // RWKV_HEAD
DECAY_LORA = 32
AAA_LORA = 32
MV_LORA = 32
GATE_LORA = 96
LNX_EPS = 64e-5
IN_SIZES = (ATTN_WIDTH, ATTN_WIDTH, ATTN_WIDTH,
            RWKV_WIDTH, RWKV_WIDTH, RWKV_WIDTH,
            2 * DECAY_LORA, 2 * AAA_LORA, GATE_LORA)
N_IN = sum(IN_SIZES)
D_FF = 2816
N_EXPERTS = 8
TOP_K = 2
D_FF_EXPERT = 3584
NORM_EPS = 1e-6

kernel_name = "hybrid_diffattn_rwkv7_moe_dit"

def _rms_norm(x, g, eps=NORM_EPS):
    xf = x.astype(jnp.float32)
    y = xf * lax.rsqrt(jnp.mean(xf * xf, axis=-1, keepdims=True) + eps)
    return y.astype(x.dtype) * g

def _split_in(p):
    return jnp.split(p, np.cumsum(IN_SIZES)[:-1].tolist(), axis=-1)

def _axial_rope_tables(n_tokens, dtype):
    rows = n_tokens // GRID_W
    row = jnp.repeat(jnp.arange(rows), GRID_W).astype(jnp.float32)
    col = jnp.tile(jnp.arange(GRID_W), rows).astype(jnp.float32)
    axis_dim = ATTN_QK_DIM // 2
    inv_freq = ROPE_THETA ** (-jnp.arange(0, axis_dim, 2, dtype=jnp.float32) / axis_dim)
    tabs = []
    for pos in (row, col):
        ang = (pos[:, None] * inv_freq[None, :])[None, :, None, None, :]
        tabs += [jnp.cos(ang).astype(dtype), jnp.sin(ang).astype(dtype)]
    return tuple(tabs)

def _rotate(x, cos, sin):
    h = x.shape[-1] // 2
    x1, x2 = x[..., :h], x[..., h:]
    return jnp.concatenate([x1 * cos - x2 * sin, x1 * sin + x2 * cos], axis=-1)

def _apply_axial_rope(x, rope):
    cos_r, sin_r, cos_c, sin_c = rope
    a = ATTN_QK_DIM // 2
    return jnp.concatenate([_rotate(x[..., :a], cos_r, sin_r),
                            _rotate(x[..., a:], cos_c, sin_c)], axis=-1)

def _diff_mix(q, keys, vals, lam):
    s = jnp.einsum("bqhmd,bkhmd->bhmqk", q, keys, preferred_element_type=jnp.float32)
    p = jax.nn.softmax(s * (ATTN_QK_DIM ** -0.5), axis=-1)
    w = p[:, :, 0] - lam * p[:, :, 1]
    return jnp.einsum("bhqk,bkhd->bqhd", w.astype(vals.dtype), vals)

def _subln(o, g, lam_init):
    b, t = o.shape[:2]
    return (_rms_norm(o, g, SUBLN_EPS) * (1.0 - lam_init)).reshape(b, t, ATTN_WIDTH)

def _diff_attention_group(pq, pk, pv, cq, ck, cv, rope, lam_p, subln_g, lam_init, need_ctx):
    b, t, _ = pq.shape

    def qk_heads(z):
        return z.reshape(z.shape[0], z.shape[1], ATTN_HEADS, 2, ATTN_QK_DIM)

    def v_heads(z):
        return z.reshape(z.shape[0], z.shape[1], ATTN_HEADS, ATTN_V_DIM)

    q = _apply_axial_rope(qk_heads(pq), rope)
    k = _apply_axial_rope(qk_heads(pk), rope)
    qc, kc, vc = qk_heads(cq), qk_heads(ck), v_heads(cv)
    lp = lam_p.astype(jnp.float32)
    lam = jnp.exp(jnp.sum(lp[0] * lp[1])) - jnp.exp(jnp.sum(lp[2] * lp[3])) + lam_init
    keys = jnp.concatenate([kc, k], axis=1)
    vals = jnp.concatenate([vc, v_heads(pv)], axis=1)
    n_blk = t // Q_BLOCK
    qb = jnp.moveaxis(q.reshape(b, n_blk, Q_BLOCK, ATTN_HEADS, 2, ATTN_QK_DIM), 1, 0)
    ob = lax.map(lambda blk: _diff_mix(blk, keys, vals, lam), qb)
    o_lat = jnp.moveaxis(ob, 0, 1).reshape(b, t, ATTN_HEADS, ATTN_V_DIM)
    out_lat = _subln(o_lat, subln_g, lam_init)
    out_ctx = _subln(_diff_mix(qc, kc, vc, lam), subln_g, lam_init) if need_ctx else None
    return out_lat, out_ctx

def _shift_mix(p, mu_prev, mu_next):
    z = jnp.zeros_like(p[:, :1])
    p_prev = jnp.concatenate([z, p[:, :-1]], axis=1)
    p_next = jnp.concatenate([p[:, 1:], z], axis=1)
    return p + mu_prev * (p_prev - p) + mu_next * (p_next - p)

def _heads(z):
    return z.reshape(z.shape[0], z.shape[1], RWKV_HEADS, RWKV_HEAD).astype(jnp.float32)

def _wkv_scan(s0, r, w, k, v, kk, a, reverse):
    def step(s, inp):
        r_t, w_t, k_t, v_t, kk_t, a_t = inp
        sa = jnp.einsum("bhvk,bhk->bhv", s, -kk_t)
        s = (s * w_t[:, :, None, :] + sa[..., None] * (kk_t * a_t)[:, :, None, :]
             + v_t[..., None] * k_t[:, :, None, :])
        return s, jnp.einsum("bhvk,bhk->bhv", s, r_t)

    xs = tuple(jnp.moveaxis(z, 1, 0) for z in (r, w, k, v, kk, a))
    s_fin, ys = lax.scan(step, s0, xs, reverse=reverse)
    return jnp.moveaxis(ys, 0, 1), s_fin

def _rwkv_prepare(seg, mu, w0, w2, a0, a2, g2, k_k, k_a, vres):
    r, k, v, wd, ad, gd = seg
    r = _shift_mix(r, mu[0, 0], mu[0, 1])
    k = _shift_mix(k, mu[1, 0], mu[1, 1])
    v = _shift_mix(v, mu[2, 0], mu[2, 1])
    if vres is not None:
        v_first, v0, v1, v2 = vres
        v = v + (v_first - v) * jax.nn.sigmoid(v0 + (v @ v1) @ v2)
    g = jax.nn.sigmoid(gd) @ g2
    kk = _heads(k * k_k)
    kk = kk * lax.rsqrt(jnp.maximum(jnp.sum(kk * kk, axis=-1, keepdims=True), 1e-24))
    kf = k.astype(jnp.float32)
    dirs = []
    for d in range(2):
        wl = (w0[d] + jnp.tanh(wd[..., d * DECAY_LORA:(d + 1) * DECAY_LORA]) @ w2[d]).astype(jnp.float32)
        decay = jnp.exp(-jnp.exp(-jax.nn.softplus(-wl) - 0.5))
        a = jax.nn.sigmoid((a0[d] + ad[..., d * AAA_LORA:(d + 1) * AAA_LORA] @ a2[d]).astype(jnp.float32))
        kd = kf * (1.0 + (a - 1.0) * k_a.astype(jnp.float32))
        dirs.append((_heads(decay), _heads(a), _heads(kd)))
    return {"r": _heads(r), "v": _heads(v), "g": g, "kk": kk, "dirs": dirs, "v_raw": v}

def _rwkv_finish(y, p, r_k, ln_w, ln_b):
    mean = jnp.mean(y, axis=-1, keepdims=True)
    var = jnp.mean(jnp.square(y - mean), axis=-1, keepdims=True)
    o = (y - mean) * lax.rsqrt(var + LNX_EPS)
    o = (o * ln_w.astype(jnp.float32).reshape(RWKV_HEADS, RWKV_HEAD)
         + ln_b.astype(jnp.float32).reshape(RWKV_HEADS, RWKV_HEAD))
    rkh = r_k.astype(jnp.float32).reshape(RWKV_HEADS, RWKV_HEAD)
    for _, _, kd in p["dirs"]:
        o = o + jnp.sum(p["r"] * kd * rkh, axis=-1, keepdims=True) * p["v"]
    b, t = o.shape[:2]
    return o.reshape(b, t, RWKV_WIDTH).astype(p["g"].dtype) * p["g"]

def _rwkv_group(seg_lat, seg_ctx, mu, w0, w2, a0, a2, g2, k_k, k_a, r_k, ln_w, ln_b, vres, need_ctx):
    if vres is None:
        vres_l = vres_c = None
    else:
        vf_l, vf_c, v0, v1, v2 = vres
        vres_l, vres_c = (vf_l, v0, v1, v2), (vf_c, v0, v1, v2)
    pl = _rwkv_prepare(seg_lat, mu, w0, w2, a0, a2, g2, k_k, k_a, vres_l)
    pc = _rwkv_prepare(seg_ctx, mu, w0, w2, a0, a2, g2, k_k, k_a, vres_c)
    b = seg_lat[0].shape[0]
    ys_l, ys_c = [], []
    for d, rev in enumerate((False, True)):
        s0 = jnp.zeros((b, RWKV_HEADS, RWKV_HEAD, RWKV_HEAD), jnp.float32)
        dc, dl = pc["dirs"][d], pl["dirs"][d]
        yc, s_ctx = _wkv_scan(s0, pc["r"], dc[0], dc[2], pc["v"], pc["kk"], dc[1], rev)
        yl, _ = _wkv_scan(s_ctx, pl["r"], dl[0], dl[2], pl["v"], pl["kk"], dl[1], rev)
        ys_l.append(yl)
        ys_c.append(yc)
    out_lat = _rwkv_finish(ys_l[0] + ys_l[1], pl, r_k, ln_w, ln_b)
    out_ctx = _rwkv_finish(ys_c[0] + ys_c[1], pc, r_k, ln_w, ln_b) if need_ctx else None
    return out_lat, out_ctx, (pl["v_raw"], pc["v_raw"])

def _swiglu(h, w1, w3, w2):
    return (jax.nn.silu(h @ w1) * (h @ w3)) @ w2

def _moe_swiglu(h, router_w, w1, w3, w2):
    shp = h.shape
    hf = h.reshape(-1, shp[-1])
    logits = jnp.matmul(hf, router_w, preferred_element_type=jnp.float32)
    top_v, top_i = lax.top_k(logits, TOP_K)
    gates = jax.nn.softmax(top_v, axis=-1)
    comb = jnp.sum(jax.nn.one_hot(top_i, N_EXPERTS, dtype=jnp.float32) * gates[..., None], axis=1)
    comb = comb.astype(h.dtype)
    y = jnp.zeros_like(hf)
    for e in range(N_EXPERTS):
        y = y + comb[:, e:e + 1] * _swiglu(hf, w1[e], w3[e], w2[e])
    return y.reshape(shp)

def _channel_mixer(h, l, ffn_w1, ffn_w3, ffn_w2, router_w, exp_w1, exp_w3, exp_w2):
    i = l // 2
    if l % 2 == 0:
        return _swiglu(h, ffn_w1[i], ffn_w3[i], ffn_w2[i])
    return _moe_swiglu(h, router_w[i], exp_w1[i], exp_w3[i], exp_w2[i])

def setup_inputs(seed: int = 0) -> dict:
    key = jax.random.key(seed)
    keys = iter(jax.random.split(key, 48))
    f32 = jnp.float32
    n_dense = (DEPTH + 1) // 2
    n_moe = DEPTH // 2
    D = D_MODEL

    def normal(shape, scale):
        return jax.random.normal(next(keys), shape, f32) * scale

    def uniform(shape, lo, hi):
        return jax.random.uniform(next(keys), shape, f32, lo, hi)

    return {
        "x": normal((BATCH, SEQ, D), 1.0),
        "c": normal((BATCH, D), 1.0),
        "ctx": normal((BATCH, CTX_LEN, D), 1.0),
        "c_ctx": normal((D,), 1.0),
        "ada_w": normal((DEPTH, D, 6 * D), D ** -0.5),
        "ada_b": normal((DEPTH, 6 * D), 0.01),
        "norm1_g": 1.0 + normal((DEPTH, D), 0.02),
        "norm2_g": 1.0 + normal((DEPTH, D), 0.02),
        "w_in": normal((DEPTH, D, N_IN), D ** -0.5),
        "w_out": normal((DEPTH, D, D), D ** -0.5),
        "diff_lambda": normal((DEPTH, 4, ATTN_QK_DIM), 0.1),
        "subln_g": 1.0 + normal((DEPTH, ATTN_V_DIM), 0.02),
        "rwkv_mu": uniform((DEPTH, 3, 2, RWKV_WIDTH), 0.0, 0.5),
        "rwkv_w0": uniform((DEPTH, 2, RWKV_WIDTH), -6.0, -1.0),
        "rwkv_w2": normal((DEPTH, 2, DECAY_LORA, RWKV_WIDTH), 0.1),
        "rwkv_a0": normal((DEPTH, 2, RWKV_WIDTH), 0.1),
        "rwkv_a2": normal((DEPTH, 2, AAA_LORA, RWKV_WIDTH), 0.1),
        "rwkv_v0": 1.0 + normal((DEPTH - 1, RWKV_WIDTH), 0.1),
        "rwkv_v1": normal((DEPTH - 1, RWKV_WIDTH, MV_LORA), RWKV_WIDTH ** -0.5),
        "rwkv_v2": normal((DEPTH - 1, MV_LORA, RWKV_WIDTH), 0.1),
        "rwkv_g2": normal((DEPTH, GATE_LORA, RWKV_WIDTH), GATE_LORA ** -0.5),
        "rwkv_k_k": 0.85 + normal((DEPTH, RWKV_WIDTH), 0.02),
        "rwkv_k_a": 1.0 + normal((DEPTH, RWKV_WIDTH), 0.02),
        "rwkv_r_k": normal((DEPTH, RWKV_WIDTH), 0.1),
        "lnx_w": 1.0 + normal((DEPTH, RWKV_WIDTH), 0.02),
        "lnx_b": normal((DEPTH, RWKV_WIDTH), 0.01),
        "ffn_w1": normal((n_dense, D, D_FF), D ** -0.5),
        "ffn_w3": normal((n_dense, D, D_FF), D ** -0.5),
        "ffn_w2": normal((n_dense, D_FF, D), D_FF ** -0.5),
        "router_w": normal((n_moe, D, N_EXPERTS), D ** -0.5),
        "exp_w1": normal((n_moe, N_EXPERTS, D, D_FF_EXPERT), D ** -0.5),
        "exp_w3": normal((n_moe, N_EXPERTS, D, D_FF_EXPERT), D ** -0.5),
        "exp_w2": normal((n_moe, N_EXPERTS, D_FF_EXPERT, D), D_FF_EXPERT ** -0.5),
        "final_g": 1.0 + normal((D,), 0.02),
    }

def reference(x, c, ctx, c_ctx, ada_w, ada_b, norm1_g, norm2_g, w_in, w_out,
              diff_lambda, subln_g, rwkv_mu, rwkv_w0, rwkv_w2, rwkv_a0, rwkv_a2,
              rwkv_v0, rwkv_v1, rwkv_v2, rwkv_g2, rwkv_k_k, rwkv_k_a, rwkv_r_k,
              lnx_w, lnx_b, ffn_w1, ffn_w3, ffn_w2, router_w, exp_w1, exp_w3, exp_w2,
              final_g):
    rope = _axial_rope_tables(x.shape[1], x.dtype)
    xc = ctx
    v_first = None
    for l in range(DEPTH):
        need_ctx = l < DEPTH - 1
        lam_init = 0.8 - 0.6 * math.exp(-0.3 * l)
        mod = jax.nn.silu(c) @ ada_w[l] + ada_b[l]
        mod_c = jax.nn.silu(c_ctx) @ ada_w[l] + ada_b[l]
        sh1, sc1, gt1, sh2, sc2, gt2 = jnp.split(mod[:, None, :], 6, axis=-1)
        csh1, csc1, cgt1, csh2, csc2, cgt2 = jnp.split(mod_c[None, None, :], 6, axis=-1)

        h = _rms_norm(x, norm1_g[l]) * (1.0 + sc1) + sh1
        hc = _rms_norm(xc, norm1_g[l]) * (1.0 + csc1) + csh1
        pl = _split_in(h @ w_in[l])
        pc = _split_in(hc @ w_in[l])
        att_l, att_c = _diff_attention_group(pl[0], pl[1], pl[2], pc[0], pc[1], pc[2], rope,
                                             diff_lambda[l], subln_g[l], lam_init, need_ctx)
        vres = None if l == 0 else (v_first[0], v_first[1], rwkv_v0[l - 1], rwkv_v1[l - 1], rwkv_v2[l - 1])
        rw_l, rw_c, v_raw = _rwkv_group(tuple(pl[3:]), tuple(pc[3:]), rwkv_mu[l], rwkv_w0[l], rwkv_w2[l],
                                        rwkv_a0[l], rwkv_a2[l], rwkv_g2[l], rwkv_k_k[l], rwkv_k_a[l],
                                        rwkv_r_k[l], lnx_w[l], lnx_b[l], vres, need_ctx)
        if l == 0:
            v_first = v_raw
        x = x + gt1 * (jnp.concatenate([att_l, rw_l], axis=-1) @ w_out[l])

        h = _rms_norm(x, norm2_g[l]) * (1.0 + sc2) + sh2
        x = x + gt2 * _channel_mixer(h, l, ffn_w1, ffn_w3, ffn_w2, router_w, exp_w1, exp_w3, exp_w2)

        if need_ctx:
            xc = xc + cgt1 * (jnp.concatenate([att_c, rw_c], axis=-1) @ w_out[l])
            hc = _rms_norm(xc, norm2_g[l]) * (1.0 + csc2) + csh2
            xc = xc + cgt2 * _channel_mixer(hc, l, ffn_w1, ffn_w3, ffn_w2, router_w, exp_w1, exp_w3, exp_w2)
    return _rms_norm(x, final_g)


_drawn_inputs = setup_inputs


def setup_inputs(seed=0):
    import zlib

    import numpy as np

    out = dict(_drawn_inputs(seed))
    spreads = {}
    factors = {'lnx_b': 7.682, 'final_g': 8.224}
    for name, (base, spread) in spreads.items():
        noise = np.random.default_rng([zlib.crc32(name.encode()), seed]).standard_normal(out[name].shape)
        drawn = base * np.exp(spread * noise) if base else spread * noise
        out[name] = __import__('jax').numpy.asarray(drawn.astype(out[name].dtype))
    for name, factor in factors.items():
        out[name] = (out[name] * factor).astype(out[name].dtype)
    return out
```

```python
from contextlib import ExitStack
import math

import numpy as np
import concourse.bass as bass
from concourse import mybir

F32 = mybir.dt.float32
I32 = mybir.dt.int32
ALU = mybir.AluOpType
ACT = mybir.ActivationFunctionType
AX = mybir.AxisListType

P = 128
D = 1024
DC = D // P
CTX, LAT = 256, 256
NTOK = CTX + LAT
DEPTH = 2
HALF = 512
CC = HALF // P
QK = 64
N_IN = 3296
LORA_COLS = 224
D_FF = 2816
FC = D_FF // P
N_EXP = 8
D_FFE = 3584
GRID_W = 64
CH = 64
NCH = NTOK // CH
LEVELS = 6
DECAY = math.exp(-0.5)
NORM_EPS, SUBLN_EPS, LNX_EPS = 1e-6, 1e-5, 64e-5
SLOTS = 128
MAX_ITEMS = N_EXP + (2 * LAT) // (SLOTS + 1)

C_IDENT, C_ONES, C_ONESBD, C_PERM, C_UPPER, C_IOTA = (k * P for k in range(6))
C_MASK = 6 * P
N_MASK = 2 + LEVELS
C_COS = C_MASK + 2 * N_MASK * P
C_SIN = C_COS + LAT
N_CONST = C_SIN + LAT


def constant_tables():
    t = np.zeros((P, N_CONST), np.float32)
    i = np.arange(P)
    t[:, C_IDENT:C_IDENT + P] = np.eye(P)
    t[:, C_ONES:C_ONES + P] = 1.0
    same = (i[:, None] // CH) == (i[None, :] // CH)
    t[:, C_ONESBD:C_ONESBD + P] = same
    t[:, C_PERM:C_PERM + P] = (i[:, None] ^ 16) == i[None, :]
    t[:, C_UPPER:C_UPPER + P] = i[:, None] < i[None, :]
    t[:, C_IOTA:C_IOTA + P] = i[None, :]
    s, q = i[:, None] % CH, i[None, :] % CH
    for d in range(2):
        a, b = (s, q) if d == 0 else (q, s)
        m = [a < b, a <= b] + [(a // (2 * w) == b // (2 * w)) & (a % (2 * w) < w) & (b % (2 * w) >= w)
                               for w in (2 ** k for k in range(LEVELS))]
        for k, v in enumerate(m):
            at = C_MASK + (d * N_MASK + k) * P
            t[:, at:at + P] = v & same
    tok = np.arange(LAT)
    inv = (10000.0 ** (-np.arange(0, 32, 2, dtype=np.float32) / 32)).astype(np.float32)
    dim = i % 64
    pos = np.where((dim < 32)[:, None], (tok // GRID_W)[None, :], (tok % GRID_W)[None, :]).astype(np.float32)
    ang = pos * inv[dim % 16][:, None]
    t[:, C_COS:C_COS + LAT] = np.cos(ang)
    t[:, C_SIN:C_SIN + LAT] = np.sin(ang) * np.where(dim % 32 < 16, -1.0, 1.0)[:, None]
    return t


VEC_A = [("ada_b", 96)]
VEC_B = [("norm1_g", 16), ("norm2_g", 16), ("final_g", 8), ("rwkv_w0", 16), ("rwkv_a0", 16), ("rwkv_k_k", 8),
         ("rwkv_k_a", 8), ("rwkv_r_k", 8), ("lnx_w", 8), ("lnx_b", 8), ("rwkv_v0", 4)]
VEC_C = [("rwkv_mu", 48), ("subln_g", 2), ("c", 8), ("c_ctx", 8)]
VEC_TILES = [VEC_A, VEC_B, VEC_C]


def vector_columns():
    cols, at, tiles = {}, 0, []
    for rows in VEC_TILES:
        first = at
        for name, n in rows:
            cols[name] = at
            at += n
        tiles.append((first, at - first))
    return cols, tiles, at


A_CONST = 0
A_VEC = N_CONST
A_MOD = A_VEC + 278
A_GAIN = A_MOD + DEPTH * 96
A_COL = A_GAIN + DEPTH * 32
A_H = 4000
A_X = A_H + 4096
A_Z = A_X
A_V = A_Z + 16384
A_BON = A_V + 2048
A_SG = A_BON + 2048
A_S = A_SG + 1024
A_RING = A_S + 17408
RING, SLOT = 3, 2048
ARENA = A_RING + RING * SLOT
A_RING2 = A_X + 4096
RING2, SLOT2 = 7, 4096
A_M = A_RING2 + RING2 * SLOT2
PRIME = 64

(K_LAM, K_NLAM, K_SUBG, K_MU1, K_KA1, K_EPS, K_WC, K_CS, K_SMALL) = (
    0, 2, 4, 6, 30, 38, 42, 106, 122)
SEQ_END = 138
assert A_COL + SEQ_END <= A_H, (A_COL + SEQ_END, A_H)


class Banks:

    def __init__(self, psum, full, free):
        self.psum, self.full, self.free = psum, full, free
        self.uses, self.where, self.turn = [0] * 8, {}, 0

    def take(self, pe, key):
        b = self.turn % 8
        self.turn += 1
        if self.uses[b]:
            pe.wait_ge(self.free[b], self.uses[b])
        self.uses[b] += 1
        self.where[key] = (b, self.uses[b])
        return self.psum[b]

    def fill(self, ins, key):
        ins.then_inc(self.full[self.where[key][0]], 1)

    def see(self, eng, key):
        b, n = self.where[key]
        eng.wait_ge(self.full[b], n)
        return self.psum[b]

    def done(self, ins, key):
        ins.then_inc(self.free[self.where[key][0]], 1)

    def released(self, eng, key):
        b, n = self.where[key]
        eng.wait_ge(self.free[b], n)

    def all_free(self, pe):
        for b in range(8):
            if self.uses[b]:
                pe.wait_ge(self.free[b], self.uses[b])


class Chain:

    def __init__(self, eng, sem):
        self.eng, self.sem, self.n = eng, sem, 0

    def __call__(self, ins):
        ins.then_inc(self.sem, 1)
        self.n += 1
        self.eng.wait_ge(self.sem, self.n)
        return ins


class LoopCount:

    def __init__(self, sem, base, names):
        self.sem, self.base, self.names = sem, base, list(names)
        self.per = len(self.names)

    def after(self, i, name):
        return i * self.per + (self.base + self.names.index(name) + 1)

    def before(self, i):
        return i * self.per + self.base

    def in_last(self, i, name):
        return i * self.per + (self.base - self.per + self.names.index(name) + 1)

    def end(self, n):
        return self.base + n * self.per


def loop_lists(with_y):
    lv = range(1, LEVELS)
    pe = ["NT", "N", "AZ", "BT", "KT", "VT"] + (["AB", "AK"] if with_y else [])
    for b in lv:
        pe += [f"T{b}", f"XT{b}"] + ([f"X{b}"] if b < LEVELS - 1 else [])
    pe += ["RHS", "U"] + (["Y"] if with_y else []) + ["ST"]
    dve = ["NTs", "XTm", "Xm", "XTi", "Xi", "AZ"] + (["AB", "AK"] if with_y else [])
    dve += [f"T{b}" for b in lv] + (["Y0", "Y1"] if with_y else []) + ["ST1", "ST2"]
    act = ["BT", "KT", "VT"]
    for b in lv:
        act += [f"XT{b}"] + ([f"X{b}"] if b < LEVELS - 1 else [])
    act += ["RHS", "U"]
    pool = ["LB0", "LB1", "LK0", "LK1", "LV0", "LV1", "LZ0", "LZ1"] + (["LR0", "LR1"] if with_y else [])
    pool += [f"M{b}" for b in lv]
    return pe, dve, act, pool


def hybrid_backbone(nc, inp, out, vf_dram, x_dram, stages=99, dump=None):
    ctx = ExitStack()
    with ctx:
        arena = ctx.enter_context(nc.sbuf_tensor("arena", [P, ARENA], F32))
        idx = ctx.enter_context(nc.sbuf_tensor("idx", [P, 16], I32))
        psum = [ctx.enter_context(nc.psum_tensor(f"ps{b}", [P, 512], F32))[:, :] for b in range(8)]
        named = {}

        def ev(name):
            if name not in named:
                named[name] = ctx.enter_context(nc.semaphore(name))
            return named[name]

        def at(off, *dims):
            n = int(np.prod(dims))
            v = arena[:, off:off + n]
            if len(dims) == 2:
                v = v.rearrange("p (a b) -> p a b", a=dims[0])
            if len(dims) == 3:
                v = v.rearrange("p (a b c) -> p a b c", a=dims[0], b=dims[1])
            return v

        banks = Banks(psum, [ev(f"bank_full{b}") for b in range(8)], [ev(f"bank_free{b}") for b in range(8)])
        ring_full = [ev(f"ring_full{k}") for k in range(RING)]

        cols, vec_tiles, n_vec = vector_columns()
        ident, ones, onesbd = at(C_IDENT, P), at(C_ONES, P), at(C_ONESBD, P)
        perm, upper, iota = at(C_PERM, P), at(C_UPPER, P), at(C_IOTA, P)
        masks = at(C_MASK, 2 * N_MASK, P)
        cos, sin = at(C_COS, LAT), at(C_SIN, LAT)
        vec = at(A_VEC, n_vec)
        mod = at(A_MOD, DEPTH, 48, 2)
        gain = at(A_GAIN, DEPTH * 2, DC, 2)
        col = at(A_COL, SEQ_END)
        cs = at(A_COL + K_CS, DC, 2)
        wc = at(A_COL + K_WC, 2, CC, NCH)
        epsc = {NORM_EPS: col[:, K_EPS:K_EPS + 1], SUBLN_EPS: col[:, K_EPS + 1:K_EPS + 2],
                LNX_EPS: col[:, K_EPS + 2:K_EPS + 3]}
        hT = at(A_H, DC, NTOK)
        xT = at(A_X, DC, NTOK)

        def vcol(name, k):
            return vec[:, cols[name] + k:cols[name] + k + 1]

        def mask(d, k):
            return masks[:, d * N_MASK + k:d * N_MASK + k + 1, :].broadcast_to([P, CC, P])

        def first(l):
            return 0 if l < DEPTH - 1 else CTX

        def streams(l):
            return [0, 1] if l < DEPTH - 1 else [1]

        vec_rows = [at(A_S + k * P, P) for k in range(3)]
        modrow = at(A_S + 512, DEPTH, 24 * 256)
        lamrow = at(A_S + 512 + 12288, DEPTH, 4, QK)
        lamtmp = at(A_S + 512 + 12288 + 512, QK)
        xin = at(A_Z + 4096, 4, D)
        sq = at(A_S, 4, NTOK)
        srt = at(A_S + 2048, NTOK)
        rst = at(A_S + 2560, NTOK)
        qT, kT, vtok = at(A_S, CC, NTOK), at(A_S + 2048, CC, NTOK), at(A_S + 4096, 4, HALF)
        A_T = A_S + 6144
        rm, km = at(A_T, 2, NTOK), at(A_T + 1024, 2, NTOK)
        th, ad = at(A_T + 2048, NTOK), at(A_T + 2560, NTOK)
        lw2, la2, lv2 = at(A_T + 3072, HALF), at(A_T + 3584, HALF), at(A_T + 4096, HALF)
        lv1 = at(A_T + 4608, CC, 32)
        reset = at(A_T + 4736, NTOK)
        kk = at(A_T + 5248, 2, NTOK)
        tA = [at(A_T + 6272 + k * NTOK, NTOK) for k in range(5)]
        vf = at(A_T + 8832, CC, NTOK)
        assert A_T + 8832 + 2048 <= A_RING
        sgd, g2 = at(A_SG, NTOK), at(A_SG + 512, HALF)
        vT = at(A_V, CC, NTOK)
        bon = at(A_BON, CC, NTOK)
        Za = [at(A_Z + (0 + d) * 2048, CC, NTOK) for d in range(2)]
        Ra = [at(A_Z + (2 + d) * 2048, CC, NTOK) for d in range(2)]
        Ba = [at(A_Z + (4 + d) * 2048, CC, NTOK) for d in range(2)]
        Ka = [at(A_Z + (6 + d) * 2048, CC, NTOK) for d in range(2)]
        Pm = [[at(A_T + (2 * b + m) * 512, 512) for m in range(2)] for b in range(2)]
        Wm = [at(A_T + 2048 + b * 512, 512) for b in range(2)]
        WT = [at(A_T + 3072 + b * 1024, 4, 256) for b in range(2)]
        asq = [at(A_T + 5120 + k * NTOK, NTOK) for k in range(4)]
        ast = at(A_T + 5120 + 4 * NTOK, NTOK)
        stat = at(A_T + 5120 + 5 * NTOK, 2, 8)
        names = ["Z", "R", "B", "K", "V", "NT", "MT", "AZ", "AB", "AK", "X", "XT", "T1", "BT", "KT", "VT", "S"]
        bd = [{n: at(A_S + (d * len(names) + k) * 512, CC, P) for k, n in enumerate(names)} for d in range(2)]
        for d in range(2):
            bd[d]["RHS"], bd[d]["U"] = bd[d]["T1"], bd[d]["MT"]
        fin = [at(A_S + k * NTOK, NTOK) for k in range(8)]
        ff = at(A_X + 4096, FC, NTOK)
        ffs = [at(A_S + 4096 + k * NTOK, NTOK) for k in range(2)]
        o = A_M
        htok = at(o, 2, D)
        hTe = at(o + 2048, DC, SLOTS)
        u = at(o + 3072, D_FFE)
        uT = at(o + 3072 + D_FFE, D_FFE // P, SLOTS)
        ye = at(o + 3072 + 2 * D_FFE, D)
        oo = o + 4096 + 2 * D_FFE
        Pe = at(oo, 2, SLOTS)
        Pw = at(oo + 256, 2, SLOTS)
        Pc = at(oo + 512, 2 * SLOTS)
        rt = at(oo + 768, 2, 96)
        assert oo + 768 + 192 <= ARENA, (oo + 960, ARENA)
        rw = at(o + 2048, DC, N_EXP)
        sqm = at(A_M, 4, LAT)
        rsm = at(A_M + 1024, 2, LAT)

        loads = []

        def w_src(w, r0, nr, c0, n):
            return w[r0 * P:(r0 + nr) * P, c0:c0 + n].rearrange("(k p) n -> p k n", p=P)

        for l in range(DEPTH):
            for j in range(24):
                loads.append((("ada", l, j), w_src(inp["ada_w"][l], 0, DC, 256 * j, 256), DC, 256))
        proj = [("lora", 3072, 224)]
        for hh, other in enumerate(("aq", "ak")):
            proj += [(f"r{hh}", 1536 + 256 * hh, 256), (f"k{hh}", 2048 + 256 * hh, 256),
                     (f"v{hh}", 2560 + 256 * hh, 256)]
            proj += [(f"{other}{q}", 512 * hh + 256 * q, 256) for q in range(2)]
        proj += [(f"av{hh}", 1024 + 256 * hh, 256) for hh in range(2)]
        for l in range(DEPTH):
            for key, c0, n in proj:
                loads.append(((key, l), w_src(inp["w_in"][l], 0, DC, c0, n), DC, n))
            for j in range(4):
                loads.append((("wout", l, j), w_src(inp["w_out"][l], 0, DC, 256 * j, 256), DC, 256))
            if l == 0:
                for j in range(D_FF // 256):
                    loads.append((("w1", j), w_src(inp["ffn_w1"][0], 0, DC, 256 * j, 256), DC, 256))
                    loads.append((("w3", j), w_src(inp["ffn_w3"][0], 0, DC, 256 * j, 256), DC, 256))
                for j in range(4):
                    for q, (r0, nr) in enumerate([(0, 8), (8, 8), (16, 6)]):
                        loads.append((("w2", j, q), w_src(inp["ffn_w2"][0], r0, nr, 256 * j, 256), nr, 256))
        load_at = {key: n for n, (key, *_) in enumerate(loads)}

        def ring_view(n):
            _, _, nk, nn = loads[n]
            return at(A_RING + (n % RING) * SLOT, nk, nn)

        def ring_wait(pe, key):
            n = load_at[key]
            pe.wait_ge(ring_full[n % RING], 16 * (n // RING + 1))
            return ring_view(n)

        loops = {}
        base = {(e, d): PRIME for e in ("pe", "dve", "act", "pool") for d in range(2)}
        for l in range(DEPTH):
            for s in range(2):
                with_y = s == 1 or l < DEPTH - 1
                lists = loop_lists(with_y)
                lc = {}
                for e, lst in zip(("pe", "dve", "act", "pool"), lists):
                    for d in range(2):
                        lc[e, d] = LoopCount(ev(f"chunk_{e}{d}"), base[e, d], lst)
                        base[e, d] = lc[e, d].end(NCH // 2)
                loops[l, s] = (with_y, lc)

        n_small = sum(len(t) for t in VEC_TILES) + 1
        xload_v = 16 * 4

        used_by = {}
        norm_no = {(0, 0): 0, (0, 1): 1, (1, 0): 2, (1, 1): 3, (2, 0): 4}
        w_base = [0, 16]
        LG, MX, R1, R2, CHO, SC, RI, CI, R3, R4, R5 = 0, 8, 16, 24, 32, 40, 48, 59, 70, 78, 86

        fr = range(7)
        turned = lambda head, tail: sum([[h(f) for h in head] + ([tail(f - 1)] if f else []) for f in fr], []) \
            + [tail(6)]
        item_banks = ["G0", "G1", "PC"] + turned([lambda f: f"A{f}", lambda f: f"B{f}"], lambda f: f"T{f}") \
            + ["Y0", "Y1"] + [f"C{g}" for g in range(4)]
        item_pe = item_banks[:-6] + [f"D{m}" for m in range(6)] + item_banks[-6:]
        item_act = ["G0", "G1", "PC"] + turned([lambda f: f"S{f}"], lambda f: f"T{f}") + ["Y0", "Y1"]
        item_dve = ["P0", "P1", "Pw0", "Pw1"] + sum([[f"UA{f}", f"U{f}"] for f in fr], []) \
            + sum([[f"C{g}a", f"C{g}"] for g in range(4)], [])
        item_cnt = {e: LoopCount(ev(f"item_{e}"), PRIME, lst)
                    for e, lst in (("pe", item_pe), ("act", item_act), ("dve", item_dve))}
        item_reader = {n: ("act", n) for n in item_act}
        item_reader.update({f"A{f}": ("dve", f"UA{f}") for f in fr})
        item_reader.update({f"B{f}": ("dve", f"U{f}") for f in fr})
        item_reader.update({f"C{g}": ("dve", f"C{g}") for g in range(4)})

        def mu1(l, x_, cc):
            return col[:, K_MU1 + 12 * l + 4 * x_ + cc:K_MU1 + 12 * l + 4 * x_ + cc + 1]

        def x_source(l, n):
            def wait(eng, c):
                if l == 2:
                    eng.wait_ge(ev("items_done"), 1)
                elif n == 1:
                    banks.released(eng, ("wo", l, c))
                else:
                    banks.released(eng, ("xt", c) if l == 0 else ("f2", c))
            return wait

        out_tile = at(A_H, 2, D)
        LAST = stages
        block = ctx.enter_context(nc.Block())

        @block.tensor
        def _(pe):
            mm = nc.tensor.matmul
            for d in range(2):
                pe.sem_inc(ev(f"chunk_pe{d}"), PRIME)
            pe.sem_inc(ev("item_pe"), PRIME)

            def product(key, outs):
                bank = banks.take(pe, key)
                for view, terms in outs:
                    for n, (a, b) in enumerate(terms):
                        ins = mm(view(bank), a, b, start=(n == 0), stop=(n == len(terms) - 1))
                banks.fill(ins, key)
                return ins

            def setup():
                pe.wait_ge(ev("const_in"), 16)
                pe.wait_ge(ev("vec_in"), 16 * n_small)
                for t, (c0, n) in enumerate(vec_tiles):
                    bank = banks.take(pe, ("vec", t))
                    banks.fill(nc.tensor.transpose(bank[:, 0:n], vec_rows[t][0:n, :], ident[0:n, 0:n]), ("vec", t))
                pe.wait_ge(ev("x_in"), xload_v)
                for c in range(DC):
                    bank = banks.take(pe, ("xt", c))
                    for t in range(4):
                        ins = nc.tensor.transpose(bank[:, t * P:(t + 1) * P], xin[:, t, c * P:(c + 1) * P], ident)
                    banks.fill(ins, ("xt", c))
                pe.wait_ge(ev("cs_ready"), 1)
                for l in range(DEPTH):
                    for j in range(24):
                        w = ring_wait(pe, ("ada", l, j))
                        product(("ada", l, j), [(lambda b: b[0:2, 0:256],
                                                 [(cs[:, k, :], w[:, k, :]) for k in range(DC)])])
                        used_by[("ada", l, j)] = ("ada", l, j)
                    for j in range(24):
                        banks.released(pe, ("ada", l, j))
                    bank = banks.take(pe, ("mod", l))
                    for j in range(48):
                        ins = nc.tensor.transpose(bank[:, 2 * j:2 * j + 2], modrow[0:2, l, j * P:(j + 1) * P],
                                                  ident[0:2, 0:2])
                    banks.fill(ins, ("mod", l))

            def norm(tag, n0, sqv, w):
                bank = banks.take(pe, ("norm", tag))
                for c in range(DC):
                    pe.wait_ge(ev("norm_sq"), DC * norm_no[tag] + c + 1)
                    ins = mm(bank[:, 0:w], ones, sqv[:, c % 4, 0:w], start=(c == 0), stop=(c == DC - 1))
                    if c < DC - 1:
                        ins.then_inc(ev("norm_used"), 1)
                banks.fill(ins, ("norm", tag))

            def project(l):
                t0 = first(l)
                pe.wait_ge(ev("h_ready"), norm_no[l, 0] + 1)

                def by_channel(load, tag, w, q, n, a):
                    product(tag, [(lambda b: b[0:n, a:NTOK],
                                   [(w[:, k, q:q + n], hT[:, k, a:NTOK]) for k in range(DC)])])
                    used_by[load] = tag

                w = ring_wait(pe, ("lora", l))
                by_channel(("lora", l), ("wd", l), w, 0, 64, 0)
                by_channel(("lora", l), ("ad", l), w, 64, 64, 0)
                by_channel(("lora", l), ("gd", l), w, 128, 96, t0)

                def rkv(hh):
                    for nm in "rkv":
                        w = ring_wait(pe, (f"{nm}{hh}", l))
                        for q in range(2):
                            by_channel((f"{nm}{hh}", l), (nm, l, 2 * hh + q), w, q * P, P, t0 if nm == "r" else 0)
                    for q in range(2):
                        pe.wait_ge(ev("kk_sq"), 4 * l + 2 * hh + q + 1)
                        product(("kn", l, 2 * hh + q), [(lambda b: b[:, :], [(onesbd, tA[q])])])

                def rates(cc):
                    banks.released(pe, ("wd", l))
                    banks.released(pe, ("ad", l))
                    pe.wait_ge(ev("lora_w_in"), 48 if l == 0 else 128)
                    for d in range(2):
                        r, cs_ = slice(32 * d, 32 * d + 32), slice(cc * P, (cc + 1) * P)
                        product(("wl", l, cc, d), [(lambda b: b[:, :], [(lw2[r, cs_], th[r, :])])])
                        product(("al", l, cc, d), [(lambda b: b[:, :], [(la2[r, cs_], ad[r, :])])])

                def bonus(cc):
                    pe.wait_ge(ev("bonus_in"), 4 * l + cc + 1)
                    product(("bn", l, cc), [(lambda b: b[:, t0:NTOK], [(onesbd, tA[0][:, t0:NTOK])])])

                def attn(nm, hh, a):
                    w = ring_wait(pe, (f"{nm}{hh}", l))
                    for q in range(2):
                        by_channel((f"{nm}{hh}", l), (nm, l, 2 * hh + q), w, q * P, P, a)

                rkv(0)
                rates(0)
                attn("aq", 0, t0)
                bonus(0)
                rates(1)
                attn("aq", 1, t0)
                bonus(1)
                rkv(1)
                rates(2)
                attn("ak", 0, 0)
                bonus(2)
                rates(3)
                attn("ak", 1, 0)
                bonus(3)
                for hh in range(2):
                    w = ring_wait(pe, (f"av{hh}", l))
                    for t in range(4):
                        product(("vt", l, hh, t), [
                            (lambda b: b[:, 0:256],
                             [(hT[:, k, t * P:(t + 1) * P], w[:, k, :]) for k in range(DC)])])
                    used_by[(f"av{hh}", l)] = ("vt", l, hh, 3)
                if l > 0:
                    for cc in range(CC):
                        banks.released(pe, ("v", l, cc))
                    product(("vv", l), [(lambda b: b[0:32, :], [(lv1[:, k, :], vT[:, k, :]) for k in range(CC)])])
                    banks.released(pe, ("vv", l))
                    for cc in range(CC):
                        product(("vg", l, cc), [(lambda b: b[:, :],
                                                 [(lv2[0:32, cc * P:(cc + 1) * P], th[0:32, :])])])
                for nm, dst in (("aq", qT), ("ak", kT)):
                    for cc in range(CC):
                        banks.released(pe, (nm, l, cc))
                        product(("rope", l, nm, cc), [(lambda b: b[:, 0:LAT], [(perm, dst[:, cc, CTX:NTOK])])])

            def attention(l):
                pe.wait_ge(ev("roped"), 8 * (l + 1))
                for hh in range(2):
                    for t in range(4):
                        banks.released(pe, ("vt", l, hh, t))
                units = [(s, h, qt) for s in streams(l) for h in range(CC) for qt in range(2)]

                def scores(n):
                    s, h, qt = units[n]
                    nk = CTX if s == 0 else NTOK
                    q0 = s * CTX + qt * P
                    for m in range(2):
                        r = slice(64 * m, 64 * m + 64)
                        product(("s", l, n, m), [(lambda b: b[:, 0:nk], [(qT[r, h, q0:q0 + P], kT[r, h, 0:nk])])])

                def outputs(n):
                    s, h, qt = units[n]
                    kts = 2 if s == 0 else 4
                    pe.wait_ge(ev("w_ready"), w_base[l] + n + 1)
                    bank = banks.take(pe, ("wt", l, n))
                    for kt in range(kts):
                        ins = nc.tensor.transpose(bank[:, kt * P:(kt + 1) * P], Wm[n % 2][:, kt * P:(kt + 1) * P],
                                                  ident)
                    banks.fill(ins, ("wt", l, n))
                    if qt == 1:
                        banks.released(pe, ("wt", l, n - 1))
                        banks.released(pe, ("wt", l, n))
                        ins = product(("o", l, s, h), [(lambda b: b[:, 0:256],
                                                        [(vtok[:, kt, h * P:(h + 1) * P], WT[(n // 2) % 2][:, kt, :])
                                                         for kt in range(kts)])])

                for n in range(len(units) + 1):
                    if n < len(units):
                        scores(n)
                    if n > 0:
                        outputs(n - 1)
                for h in range(CC):
                    for s in streams(l):
                        banks.released(pe, ("o", l, s, h))
                    t0 = first(l)
                    product(("on", l, h), [(lambda b: b[:, t0:NTOK], [(ones, asq[h][:, t0:NTOK])])])

            def chunks(l, s):
                with_y, lc = loops[l, s]
                pl = lc["pe", 0].names
                banks.all_free(pe)

                operands = {
                    "NT": [("B", "Z")], "N": [("Z", "B")], "AZ": [("K", "Z")], "AB": [("B", "R")],
                    "AK": [("K", "R")], "RHS": [("Z", "S"), ("AZ", "VT")], "U": [("XT", "RHS")],
                    "Y": [("S", "R"), ("U", "AB"), ("VT", "AK")], "ST": [("BT", "U"), ("KT", "VT")],
                }
                for b in range(1, LEVELS):
                    operands[f"T{b}"] = [("MT", "X")]
                    operands[f"XT{b}"] = [("T1", "XT")]
                    operands[f"X{b}"] = [("XT", "T1")]
                needs = {
                    "NT": [("pool", "LZ1")], "N": [], "AZ": [], "BT": [], "KT": [], "VT": [],
                    "AB": [("pool", "LR1")] if with_y else [], "AK": [],
                    "RHS": [("dve", "AZ"), ("act", "VT")], "U": [("act", "RHS"), ("act", f"XT{LEVELS - 1}")],
                    "Y": [("act", "U")], "ST": [("act", "U"), ("act", "KT"), ("act", "BT")],
                }
                if with_y:
                    needs["Y"] += [("dve", "AK")]
                for b in range(1, LEVELS):
                    needs[f"T{b}"] = [("pool", f"M{b}")] + ([("dve", "Xi")] if b == 1 else [("act", f"X{b - 1}")])
                    needs[f"XT{b}"] = [("dve", f"T{b}")] + ([("dve", "XTi")] if b == 1 else [("act", f"XT{b - 1}")])
                    needs[f"X{b}"] = []
                reader = {"NT": ("dve", "XTm"), "N": ("dve", "Xm"), "Y": ("dve", "Y1"), "ST": ("dve", "ST1")}
                for nme in pl:
                    if nme not in reader:
                        reader[nme] = ("dve", nme) if nme in lc["dve", 0].names else ("act", nme)
                        assert nme in lc[reader[nme][0], 0].names

                with pe.Fori(0, NCH // 2) as i:
                    for pos, nme in enumerate(pl):
                        for d in range(2):
                            cnt = {e: lc[e, d] for e in ("pe", "dve", "act", "pool")}
                            if pos == 0:
                                pe.wait_ge(cnt["dve"].sem, cnt["dve"].before(i))
                                pe.wait_ge(cnt["act"].sem, cnt["act"].before(i))
                            want = list(needs[nme])
                            if pos >= 4:
                                want.append(reader[pl[pos - 4]])
                            for e in ("pool", "dve", "act"):
                                steps = [step for x_, step in want if x_ == e]
                                if steps:
                                    pe.wait_ge(cnt[e].sem, cnt[e].after(i, max(steps, key=cnt[e].names.index)))
                            bank = psum[4 * d + pos % 4]
                            for cc in range(CC):
                                view = bank[:, cc * P:(cc + 1) * P]
                                if nme in ("BT", "KT", "VT"):
                                    ins = nc.tensor.transpose(view, bd[d][nme[0]][:, cc, :], ident)
                                else:
                                    terms = operands[nme]
                                    for n, (a, b) in enumerate(terms):
                                        ins = mm(view, bd[d][a][:, cc, :], bd[d][b][:, cc, :],
                                                 start=(n == 0), stop=(n == len(terms) - 1))
                            ins.then_inc(cnt["pe"].sem, 1)
                for d in range(2):
                    for e in ("dve", "act"):
                        pe.wait_ge(lc[e, d].sem, lc[e, d].end(NCH // 2))

            def finish(l):
                t0 = first(l)
                for cc in range(CC):
                    product(("ym", l, cc), [(lambda b: b[:, t0:NTOK], [(onesbd, hT[:, 4 + cc, t0:NTOK])])])
                for cc in range(CC):
                    pe.wait_ge(ev("y_sq"), 4 * l + cc + 1)
                    product(("yv", l, cc), [(lambda b: b[:, t0:NTOK], [(onesbd, fin[cc][:, t0:NTOK])])])
                    product(("yg", l, cc), [(lambda b: b[:, t0:NTOK],
                                             [(g2[0:96, cc * P:(cc + 1) * P], sgd[0:96, t0:NTOK])])])

            def w_out(l):
                t0 = first(l)
                for cc in range(CC):
                    banks.released(pe, ("yg", l, cc))
                pe.wait_ge(ev("att_normed"), 4 * (l + 1))
                for j in range(4):
                    w = ring_wait(pe, ("wout", l, j))
                    for q in range(2):
                        product(("wo", l, 2 * j + q), [
                            (lambda b: b[:, t0:NTOK],
                             [(w[:, k, q * P:(q + 1) * P], hT[:, k, t0:NTOK]) for k in range(DC)])])
                    used_by[("wout", l, j)] = ("wo", l, 2 * j + 1)

            def feed_forward():
                pe.wait_ge(ev("h_ready"), norm_no[0, 1] + 1)
                for j in range(D_FF // 256):
                    for nm in ("w1", "w3"):
                        w = ring_wait(pe, (nm, j))
                        for q in range(2):
                            product((nm, 2 * j + q), [(lambda b: b[:, :], [
                                (w[:, k, q * P:(q + 1) * P], hT[:, k, :]) for k in range(DC)])])
                        used_by[(nm, j)] = (nm, 2 * j + 1)
                for j in range(4):
                    pair = [banks.take(pe, ("f2", 2 * j + q)) for q in range(2)]
                    k0 = 0
                    for part, nr in enumerate((8, 8, 6)):
                        w = ring_wait(pe, ("w2", j, part))
                        for q in range(2):
                            for k in range(nr):
                                if j == 0 and q == 0:
                                    banks.released(pe, ("w3", k0 + k))
                                ins = mm(pair[q][:, :], w[:, k, q * P:(q + 1) * P], ff[:, k0 + k, :],
                                         start=(k0 + k == 0), stop=(k0 + k == FC - 1))
                            if part == 2:
                                banks.fill(ins, ("f2", 2 * j + q))
                        if part < 2:
                            ins.then_inc(ev("w2_part"), 1)
                        used_by[("w2", j, part)] = ("f2", 2 * j + 1) if part == 2 else 2 * j + part + 1
                        k0 += nr

            def route():
                pe.wait_ge(ev("h_ready"), norm_no[1, 1] + 1)
                pe.wait_ge(ev("router_in"), 16)
                for t in range(2):
                    for half in range(2):
                        bank = banks.take(pe, ("ht", t, half))
                        for c in range(4):
                            ins = nc.tensor.transpose(bank[:, c * P:(c + 1) * P],
                                                      hT[:, 4 * half + c, CTX + t * P:CTX + (t + 1) * P], ident)
                        banks.fill(ins, ("ht", t, half))
                for t in range(2):
                    product(("lg", t), [(lambda b: b[:, 0:8], [
                        (hT[:, k, CTX + t * P:CTX + (t + 1) * P], rw[:, k, :]) for k in range(DC)])])
                pe.wait_ge(ev("chosen"), 2)
                ch = [rt[:, t, CHO:CHO + 8] for t in range(2)]
                product(("rk", 0), [(lambda b: b[:, 0:8], [(upper, ch[0])])])
                product(("rk", 1), [(lambda b: b[:, 0:8], [(upper, ch[1]), (ones, ch[0])])])
                product(("ct", 0), [(lambda b: b[:, 0:8], [(ones, ch[0]), (ones, ch[1])])])

            def experts():
                banks.all_free(pe)
                pe.wait_ge(ev("items_ready"), 1)
                T = pe.value_load(idx[0:1, 15:16], min_val=N_EXP, max_val=MAX_ITEMS)
                cnt = item_cnt
                with pe.Fori(0, T) as i:
                    def wait(e, step):
                        pe.wait_ge(cnt[e].sem, cnt[e].after(i, step))

                    def w_wait(m):
                        pe.wait_ge(ev(f"ring2_full{m % RING2}"), i * 48 + 16 * (m // RING2 + 1))
                        return at(A_RING2 + (m % RING2) * SLOT2, SLOT2)

                    def bank_of(nme):
                        pos = item_banks.index(nme)
                        if pos >= 8:
                            wait(*item_reader[item_banks[pos - 8]])
                        return psum[pos % 8]

                    pe.wait_ge(cnt["dve"].sem, cnt["dve"].before(i))
                    pe.wait_ge(cnt["act"].sem, cnt["act"].before(i))
                    wait("dve", "P1")
                    for g in range(2):
                        bank = bank_of(f"G{g}")
                        for c in range(4):
                            for t in range(2):
                                k = 4 * g + c
                                ins = mm(bank[:, c * P:(c + 1) * P], htok[:, t, k * P:(k + 1) * P], Pe[:, t, :],
                                         start=(t == 0), stop=(t == 1))
                        ins.then_inc(cnt["pe"].sem, 1)
                    wait("dve", "Pw1")
                    bank = bank_of("PC")
                    for t in range(2):
                        ins = nc.tensor.transpose(bank[:, t * P:(t + 1) * P], Pw[:, t, :], ident)
                    ins.then_inc(cnt["pe"].sem, 1)
                    wait("act", "G1")

                    def turn(f):
                        wait("dve", f"U{f}")
                        bank = bank_of(f"T{f}")
                        for q in range(4):
                            k = 4 * f + q
                            ins = nc.tensor.transpose(bank[:, q * P:(q + 1) * P], u[:, k * P:(k + 1) * P], ident)
                        ins.then_inc(cnt["pe"].sem, 1)

                    for f in range(7):
                        for x_, nme in enumerate((f"A{f}", f"B{f}")):
                            w = w_wait(2 * f + x_).rearrange("p (k n) -> p k n", k=DC)
                            bank = bank_of(nme)
                            for k in range(DC):
                                ins = mm(bank[:, :], hTe[:, k, :], w[:, k, :], start=(k == 0), stop=(k == DC - 1))
                            ins.then_inc(cnt["pe"].sem, 1)
                        if f:
                            turn(f - 1)
                    turn(6)
                    b0, b1 = bank_of("Y0"), bank_of("Y1")
                    for m in range(7):
                        wait("act", f"T{m}")
                        w = w_wait(14 + m).rearrange("p (k n) -> p k n", k=4)
                        for half, bank in enumerate((b0, b1)):
                            for q in range(4):
                                k = 4 * m + q
                                ins = mm(bank[:, :], uT[:, k, :], w[:, q, half * 512:(half + 1) * 512],
                                         start=(k == 0), stop=(k == 27))
                            if m == 6:
                                ins.then_inc(cnt["pe"].sem, 1)
                        if m < 6:
                            ins.then_inc(cnt["pe"].sem, 1)
                    wait("act", "Y1")
                    wait("act", "PC")
                    for g in range(4):
                        bank = bank_of(f"C{g}")
                        for q in range(2):
                            c = 2 * g + q
                            ins = mm(bank[:, q * 256:(q + 1) * 256], ye[:, c * P:(c + 1) * P], Pc, start=True,
                                     stop=True)
                        ins.then_inc(cnt["pe"].sem, 1)
                pe.wait_ge(ev("items_done"), 1)

            def final():
                for t in range(2):
                    for half in range(2):
                        bank = banks.take(pe, ("fin", t, half))
                        if t == 0 and half == 0:
                            pe.wait_ge(ev("out_scaled"), 1)
                        for c in range(4):
                            ins = nc.tensor.transpose(bank[:, c * P:(c + 1) * P],
                                                      xT[:, 4 * half + c, CTX + t * P:CTX + (t + 1) * P], ident)
                        banks.fill(ins, ("fin", t, half))

            seq = [setup]
            for l in range(DEPTH):
                seq += [lambda l=l: norm((l, 0), 0, sq, NTOK), lambda l=l: project(l), lambda l=l: attention(l),
                        lambda l=l: chunks(l, 0), lambda l=l: chunks(l, 1), lambda l=l: finish(l),
                        lambda l=l: w_out(l)]
                if l == 0:
                    seq += [lambda: norm((0, 1), 0, sq, NTOK), feed_forward]
                else:
                    seq += [lambda: norm((1, 1), CTX, sqm, LAT), route, experts]
            seq += [lambda: norm((2, 0), CTX, sqm, LAT), final]
            for f in seq[:LAST]:
                f()

        @block.scalar
        def _(act):
            f_ = nc.scalar.activation
            chain = Chain(act, ev("act_chain"))
            for d in range(2):
                act.sem_inc(ev(f"chunk_act{d}"), PRIME)
            act.sem_inc(ev("item_act"), PRIME)

            def copy_out(key, dst, src, scale=1.0, func=ACT.Copy, bias=0.0):
                bank = banks.see(act, key)
                ins = f_(dst, src(bank), func, bias=bias, scale=scale)
                banks.done(ins, key)
                return ins

            def setup():
                act.dma_start(arena[:, 0:N_CONST], inp["const_tables"]).then_inc(ev("const_in"), 16)
                act.dma_start(lamrow.rearrange("p a b c -> p (a b c)"),
                              inp["diff_lambda"].rearrange("l a b -> (l a b)").partition_broadcast(P)
                              ).then_inc(ev("vec_in"), 16)
                for t, tile in enumerate(VEC_TILES):
                    r = 0
                    for name, n in tile:
                        src = inp[name]
                        nd = len(src.shape)
                        flat = {1: "d -> (d)", 2: "a d -> (a d)", 3: "a b d -> (a b d)", 4: "a b e d -> (a b e d)"}
                        src = src.rearrange(flat[nd]) if nd > 1 else src
                        act.dma_start(vec_rows[t][r:r + n, :], src.rearrange("(n p) -> n p", p=P)
                                      ).then_inc(ev("vec_in"), 16)
                        r += n
                for k, src in enumerate((inp["ctx"][0], inp["x"][0])):
                    for t in range(2):
                        act.dma_start(xin[:, 2 * k + t, :], src[t * P:(t + 1) * P, :]).then_inc(ev("x_in"), 16)
                act.wait_ge(ev("vec_cols"), 1)
                f_(col[:, K_SMALL:K_SMALL + 16], vec[:, cols["c"]:cols["c"] + 16], ACT.Sigmoid
                   ).then_inc(ev("c_sig"), 1)
                act.wait_ge(ev("lam_sums"), 1)
                f_(col[:, K_SMALL:K_SMALL + 4], col[:, K_SMALL:K_SMALL + 4], ACT.Exp).then_inc(ev("lam_exp"), 1)
                for l in range(DEPTH):
                    for j in range(24):
                        copy_out(("ada", l, j), modrow[0:2, l, j * 256:(j + 1) * 256], lambda b: b[0:2, 0:256])

            def norm(tag, c0, sqv, srtv, source):
                no = norm_no[tag]
                w = NTOK - c0
                for c in range(DC):
                    source(act, c)
                    if c >= 4:
                        act.wait_ge(ev("norm_used"), (DC - 1) * no + c - 3)
                    f_(sqv[:, c % 4, 0:w], xT[:, c, c0:NTOK], ACT.Square).then_inc(ev("norm_sq"), 1)
                bank = banks.see(act, ("norm", tag))
                banks.done(f_(srtv[:, 0:w], bank[:, 0:w], ACT.Sqrt, bias=epsc[NORM_EPS], scale=1.0 / D),
                           ("norm", tag))
                if tag[0] == 2:
                    return
                if tag[1] == 0:
                    act.dma_start(x_dram, xT.rearrange("p a b -> p (a b)")).then_inc(ev("x_parked"), 16)
                l, n = tag
                for c in range(DC):
                    act.wait_ge(ev("h_scaled"), DC * no + c + 1)
                    for s in (streams(l) if n else [0, 1]):
                        r = slice(s * CTX, s * CTX + CTX)
                        ins = f_(hT[:, c, r], hT[:, c, r], ACT.Identity, bias=mod[:, l, 24 * n + c, s:s + 1])
                ins.then_inc(ev("h_ready"), 1)

            def project(l):
                t0 = first(l)
                if l > 0:
                    act.wait_ge(ev("vf_out"), 16)
                    act.dma_start(vf.rearrange("p a b -> p (a b)"), vf_dram).then_inc(ev("vf_in"), 16)
                copy_out(("wd", l), th[0:64, :], lambda b: b[0:64, :], func=ACT.Tanh)
                copy_out(("ad", l), ad[0:64, :], lambda b: b[0:64, :])
                copy_out(("gd", l), sgd[0:96, t0:NTOK], lambda b: b[0:96, t0:NTOK], func=ACT.Sigmoid)

                def rkv(hh):
                    if hh:
                        act.wait_ge(ev("bonus_in"), 4 * l + 2)
                        banks.see(act, ("bn", l, 1))
                    for x_, nm in enumerate("rkv"):
                        a = t0 if nm == "r" else 0
                        for q in range(2):
                            cc = 2 * hh + q
                            dst = vT[:, cc] if nm == "v" else (rm, km)[x_][:, q]
                            bank = banks.see(act, (nm, l, cc))
                            f_(dst[:, a:NTOK], bank[:, a:NTOK], ACT.Copy, scale=mu1(l, x_, cc)
                               ).then_inc(ev("mix_self"), 1)
                    for q in range(2):
                        cc = 2 * hh + q
                        banks.released(act, ("k", l, cc))
                        chain(f_(kk[:, q], km[:, q], ACT.Copy, scale=vcol("rwkv_k_k", 4 * l + cc)))
                        f_(tA[q], kk[:, q], ACT.Square).then_inc(ev("kk_sq"), 1)
                    for q in range(2):
                        banks.released(act, ("kn", l, 2 * hh + q))
                        f_(tA[q], tA[q], ACT.Sqrt).then_inc(ev("kn_root"), 1)

                def rates(cc):
                    act.wait_ge(ev("kk_ready"), 4 * l + 2 * (cc // 2) + 2)
                    if cc:
                        banks.see(act, ("bn", l, cc - 1))
                    if cc == 0:
                        act.wait_ge(ev("x_parked"), 16 * (l + 1))
                    for d in range(2):
                        no = 8 * l + 2 * cc + d
                        if d:
                            act.wait_ge(ev("rates_used"), no)
                        copy_out(("wl", l, cc, d), tA[0], lambda b: b, func=ACT.Sigmoid,
                                 bias=vcol("rwkv_w0", 8 * l + 4 * d + cc))
                        copy_out(("al", l, cc, d), tA[1], lambda b: b, func=ACT.Sigmoid,
                                 bias=vcol("rwkv_a0", 8 * l + 4 * d + cc))
                        act.wait_ge(ev("sums_ready"), no + 1)
                        incl, excl = (tA[2], tA[3])
                        f_(Ba[d][:, cc], incl, ACT.Exp, scale=DECAY)
                        f_(Ka[d][:, cc], incl, ACT.Exp, scale=DECAY)
                        f_(Ra[d][:, cc], incl, ACT.Exp, scale=-DECAY)
                        f_(wc[:, d, cc, :], wc[:, d, cc, :], ACT.Exp, scale=-DECAY)
                        f_(Za[d][:, cc], excl, ACT.Exp, scale=-DECAY).then_inc(ev("decays"), 1)

                def attn(nm, hh, dst, a):
                    for q in range(2):
                        copy_out((nm, l, 2 * hh + q), dst[:, 2 * hh + q, a:NTOK], lambda b: b[:, a:NTOK])

                rkv(0)
                rates(0)
                attn("aq", 0, qT, t0)
                rates(1)
                attn("aq", 1, qT, t0)
                rkv(1)
                rates(2)
                attn("ak", 0, kT, 0)
                rates(3)
                attn("ak", 1, kT, 0)
                if l == 0:
                    for cc in range(CC):
                        banks.released(act, ("v", l, cc))
                    act.dma_start(vf_dram, vT.rearrange("p a b -> p (a b)")).then_inc(ev("vf_out"), 16)
                for hh in range(2):
                    for t in range(4):
                        copy_out(("vt", l, hh, t), vtok[:, t, hh * 256:(hh + 1) * 256], lambda b: b[:, 0:256])
                if l > 0:
                    copy_out(("vv", l), th[0:32, :], lambda b: b[0:32, :])
                    act.wait_ge(ev("rates_used"), 8 * (l + 1))
                    banks.see(act, ("bn", l, 3))
                    for cc in range(CC):
                        copy_out(("vg", l, cc), tA[cc], lambda b: b, func=ACT.Sigmoid, bias=vcol("rwkv_v0", cc))

            def attention(l):
                units = [(s, h, qt) for s in streams(l) for h in range(CC) for qt in range(2)]
                for n in range(len(units) + 1):
                    if n < len(units):
                        nk = CTX if units[n][0] == 0 else NTOK
                        act.wait_ge(ev("max_ready"), w_base[l] + n + 1)
                        for m in range(2):
                            if n >= 2:
                                act.wait_ge(ev("w_ready"), w_base[l] + n - 1)
                            bank = banks.see(act, ("s", l, n, m))
                            banks.done(f_(Pm[n % 2][m][:, 0:nk], bank[:, 0:nk], ACT.Exp,
                                          bias=stat[:, n % 2, 2 + m:3 + m], scale=QK ** -0.5,
                                          accum_out=stat[:, n % 2, 4 + m:5 + m]), ("s", l, n, m))
                    if n > 0:
                        s, h, qt = units[n - 1]
                        kts = 2 if s == 0 else 4
                        copy_out(("wt", l, n - 1), WT[((n - 1) // 2) % 2][:, 0:kts, qt * P:(qt + 1) * P],
                                 lambda b: b[:, 0:kts * P].rearrange("p (a b) -> p a b", a=kts))
                        if qt == 1:
                            r = slice(s * CTX, (s + 1) * CTX)
                            bank = banks.see(act, ("o", l, s, h))
                            f_(hT[:, h, r], bank[:, 0:256], ACT.Copy)
                            banks.done(f_(asq[h][:, r], bank[:, 0:256], ACT.Square), ("o", l, s, h))
                t0 = first(l)
                for h in range(CC):
                    copy_out(("on", l, h), asq[h][:, t0:NTOK], lambda b: b[:, t0:NTOK], func=ACT.Sqrt,
                             bias=epsc[SUBLN_EPS], scale=1.0 / P)

            def chunks(l, s):
                with_y, lc = loops[l, s]
                with act.Fori(0, NCH // 2) as i:
                    for nme in lc["act", 0].names:
                        for d in range(2):
                            pe_c, own = lc["pe", d], lc["act", d]
                            seen = nme
                            if nme.startswith("XT") and nme != f"XT{LEVELS - 1}":
                                seen = "X" + nme[2:]
                            act.wait_ge(pe_c.sem, pe_c.after(i, seen))
                            bank = psum[4 * d + pe_c.names.index(nme) % 4]
                            dst = bd[d][nme.rstrip("12345") if nme[0] == "X" else nme]
                            f_(dst.rearrange("p a b -> p (a b)"), bank, ACT.Copy).then_inc(own.sem, 1)

            def finish(l):
                t0 = first(l)
                for d in range(2):
                    c_ = loops[l, 1][1]["pe", d]
                    act.wait_ge(c_.sem, c_.end(NCH // 2))
                    g_ = loops[l, 1][1]["pool", d]
                    act.wait_ge(g_.sem, g_.end(NCH // 2))
                act.dma_start(xT.rearrange("p a b -> p (a b)"), x_dram).then_inc(ev("x_back"), 16)
                for cc in range(CC):
                    banks.released(act, ("ym", l, cc))
                    f_(fin[cc][:, t0:NTOK], hT[:, 4 + cc, t0:NTOK], ACT.Square).then_inc(ev("y_sq"), 1)
                for cc in range(CC):
                    copy_out(("yv", l, cc), fin[cc][:, t0:NTOK], lambda b: b[:, t0:NTOK], func=ACT.Sqrt,
                             bias=epsc[LNX_EPS], scale=1.0 / CH)

            def feed_forward():
                for c in range(FC):
                    bank = banks.see(act, ("w1", c))
                    if c >= 2:
                        banks.released(act, ("w3", c - 2))
                    f_(ffs[c % 2], bank, ACT.Sigmoid).then_inc(ev("ff_sig"), 1)

            def route():
                for t in range(2):
                    for half in range(2):
                        copy_out(("ht", t, half), htok[:, t, half * 512:(half + 1) * 512], lambda b: b)
                act.wait_ge(ev("gate_in"), 1)
                for t in range(2):
                    ins = f_(rt[:, t, SC + 1:SC + 2], rt[:, t, SC:SC + 1], ACT.Exp)
                ins.then_inc(ev("gate_exp"), 1)

            def experts():
                act.wait_ge(ev("items_ready"), 1)
                T = act.value_load(idx[0:1, 15:16], min_val=N_EXP, max_val=MAX_ITEMS)
                cnt = item_cnt
                with act.Fori(0, T) as i:
                    for nme in item_act:
                        act.wait_ge(cnt["pe"].sem, cnt["pe"].after(i, nme if nme[0] != "S" else "A" + nme[1:]))
                        src = psum[item_banks.index(nme if nme[0] != "S" else "A" + nme[1:]) % 8]
                        k = int(nme[1:]) if nme != "PC" else 0
                        if nme[0] == "G":
                            dst, src, fn = hTe[:, 4 * k:4 * k + 4, :].rearrange("p a b -> p (a b)"), src, ACT.Copy
                        elif nme == "PC":
                            dst, src, fn = Pc, src[:, 0:256], ACT.Copy
                        elif nme[0] == "S":
                            dst, fn = u[:, k * 512:(k + 1) * 512], ACT.Sigmoid
                        elif nme[0] == "T":
                            dst, fn = uT[:, 4 * k:4 * k + 4, :].rearrange("p a b -> p (a b)"), ACT.Copy
                        else:
                            dst, fn = ye[:, k * 512:(k + 1) * 512], ACT.Copy
                        f_(dst, src, fn).then_inc(cnt["act"].sem, 1)

            seq = [setup]
            for l in range(DEPTH):
                seq += [lambda l=l: norm((l, 0), 0, sq, srt, x_source(l, 0)), lambda l=l: project(l),
                        lambda l=l: attention(l), lambda l=l: chunks(l, 0), lambda l=l: chunks(l, 1),
                        lambda l=l: finish(l), lambda: None]
                if l == 0:
                    seq += [lambda: norm((0, 1), 0, sq, srt, x_source(0, 1)), feed_forward]
                else:
                    seq += [lambda: norm((1, 1), CTX, sqm, rsm[:, 0], x_source(1, 1)), route, experts]
            seq += [lambda: norm((2, 0), CTX, sqm, rsm[:, 0], x_source(2, 0)), lambda: None]
            for f in seq[:LAST]:
                f()

        @block.vector
        def _(dve):
            v = nc.vector
            chain = Chain(dve, ev("dve_chain"))
            for d in range(2):
                dve.sem_inc(ev(f"chunk_dve{d}"), PRIME)
            dve.sem_inc(ev("item_dve"), PRIME)

            def setup():
                for k, eps in enumerate((NORM_EPS, SUBLN_EPS, LNX_EPS)):
                    chain(v.memset(col[:, K_EPS + k:K_EPS + k + 1], eps))
                for t, (c0, n) in enumerate(vec_tiles):
                    bank = banks.see(dve, ("vec", t))
                    banks.done(v.tensor_copy(vec[:, c0:c0 + n], bank[:, 0:n]), ("vec", t))
                for t in range(3):
                    banks.released(dve, ("vec", t))
                chain(v.memset(col[:, K_SMALL + 15:K_SMALL + 16], 0.0))
                dve.sem_inc(ev("vec_cols"), 1)
                dve.wait_ge(ev("c_sig"), 1)
                cvec, csig = vec[:, cols["c"]:cols["c"] + 16], col[:, K_SMALL:K_SMALL + 16]
                chain(v.tensor_tensor(cs[:, :, 1], cvec[:, 0:8], csig[:, 0:8], ALU.mult))
                v.tensor_tensor(cs[:, :, 0], cvec[:, 8:16], csig[:, 8:16], ALU.mult).then_inc(ev("cs_ready"), 1)
                dve.wait_ge(ev("cs_ready"), 1)
                for l in range(DEPTH):
                    for k in range(2):
                        chain(v.tensor_tensor_reduce(lamtmp, lamrow[:, l, 2 * k, :], lamrow[:, l, 2 * k + 1, :], 1.0,
                                                     0.0, ALU.mult, ALU.add,
                                                     col[:, K_SMALL + 2 * l + k:K_SMALL + 2 * l + k + 1]))
                dve.sem_inc(ev("lam_sums"), 1)
                dve.wait_ge(ev("lam_exp"), 1)
                for l in range(DEPTH):
                    lam_init = 0.8 - 0.6 * math.exp(-0.3 * l)
                    e = col[:, K_SMALL + 2 * l:K_SMALL + 2 * l + 2]
                    chain(v.tensor_tensor(col[:, K_LAM + l:K_LAM + l + 1], e[:, 0:1], e[:, 1:2], ALU.subtract))
                    chain(v.tensor_scalar(col[:, K_NLAM + l:K_NLAM + l + 1], col[:, K_LAM + l:K_LAM + l + 1],
                                          lam_init, -1.0, ALU.add, ALU.mult))
                    chain(v.tensor_scalar(col[:, K_SUBG + l:K_SUBG + l + 1], vcol("subln_g", l), 1.0 - lam_init, None,
                                          ALU.mult))
                    for x_ in range(3):
                        c0 = K_MU1 + 12 * l + 4 * x_
                        m0 = cols["rwkv_mu"] + (l * 3 + x_) * 8
                        chain(v.tensor_tensor(col[:, c0:c0 + 4], vec[:, m0:m0 + 4], vec[:, m0 + 4:m0 + 8], ALU.add))
                        chain(v.tensor_scalar(col[:, c0:c0 + 4], col[:, c0:c0 + 4], -1.0, 1.0, ALU.mult, ALU.add))
                    chain(v.tensor_scalar(col[:, K_KA1 + 4 * l:K_KA1 + 4 * l + 4],
                                          vec[:, cols["rwkv_k_a"] + 4 * l:cols["rwkv_k_a"] + 4 * l + 4], -1.0, 1.0,
                                          ALU.mult, ALU.add))
                dve.sem_inc(ev("cols_ready"), 1)
                for c in range(DC):
                    bank = banks.see(dve, ("xt", c))
                    banks.done(v.tensor_copy(xT[:, c, :], bank), ("xt", c))
                for l in range(DEPTH):
                    bank = banks.see(dve, ("mod", l))
                    c0 = cols["ada_b"] + 48 * l
                    banks.done(v.tensor_tensor(mod[:, l, :, :], bank[:, 0:96].rearrange("p (a b) -> p a b", b=2),
                                               vec[:, c0:c0 + 48].unsqueeze(2).broadcast_to([P, 48, 2]), ALU.add),
                               ("mod", l))
                    banks.released(dve, ("mod", l))
                    for n in range(2):
                        c0 = cols[f"norm{n + 1}_g"] + 8 * l
                        chain(v.scalar_tensor_tensor(
                            gain[:, 2 * l + n, :, :], mod[:, l, 24 * n + 8:24 * n + 16, :], 1.0,
                            vec[:, c0:c0 + 8].unsqueeze(2).broadcast_to([P, 8, 2]), ALU.add, ALU.mult))

            def norm(tag, c0, srtv, rstv):
                w = NTOK - c0
                banks.released(dve, ("norm", tag))
                chain(v.reciprocal(rstv[:, 0:w], srtv[:, 0:w]))
                l, n = tag
                for c in range(DC):
                    if l == 2:
                        ins = v.scalar_tensor_tensor(xT[:, c, c0:NTOK], xT[:, c, c0:NTOK], vcol("final_g", c),
                                                     rstv[:, 0:w], ALU.mult, ALU.mult)
                        continue
                    for s in (streams(l) if n else [0, 1]):
                        r = slice(s * CTX, (s + 1) * CTX)
                        ro = slice(s * CTX - c0, (s + 1) * CTX - c0)
                        ins = v.scalar_tensor_tensor(hT[:, c, r], xT[:, c, r], gain[:, 2 * l + n, c, s:s + 1],
                                                     rstv[:, ro], ALU.mult, ALU.mult)
                    ins.then_inc(ev("h_scaled"), 1)
                if l == 2:
                    ins.then_inc(ev("out_scaled"), 1)

            def project(l):
                t0 = first(l)

                def mix(nm, x_, cc, q, no):
                    dst = vT[:, cc] if nm == "v" else (rm, km)[x_][:, q]
                    bank = banks.see(dve, (nm, l, cc))
                    ss = streams(l) if nm == "r" else [0, 1]
                    a, n = ss[0] * CTX, len(ss)
                    dv_ = dst[:, a:NTOK].rearrange("p (s t) -> p s t", s=n)
                    pv = bank[:, a:NTOK].rearrange("p (s t) -> p s t", s=n)
                    m0 = (l * 3 + x_) * 8 + cc
                    dve.wait_ge(ev("mix_self"), no)
                    chain(v.scalar_tensor_tensor(dv_[:, :, 1:CTX], pv[:, :, 0:CTX - 1], vcol("rwkv_mu", m0),
                                                 dv_[:, :, 1:CTX], ALU.mult, ALU.add))
                    banks.done(v.scalar_tensor_tensor(dv_[:, :, 0:CTX - 1], pv[:, :, 1:CTX],
                                                      vcol("rwkv_mu", m0 + 4), dv_[:, :, 0:CTX - 1], ALU.mult,
                                                      ALU.add), (nm, l, cc))

                def rkv(hh):
                    no = 12 * l + 6 * hh
                    for x_, nm in enumerate("rkv"):
                        for q in range(2):
                            no += 1
                            mix(nm, x_, 2 * hh + q, q, no)
                    for q in range(2):
                        bank = banks.see(dve, ("kn", l, 2 * hh + q))
                        banks.done(v.tensor_scalar(tA[q], bank, 1e-24, None, ALU.max), ("kn", l, 2 * hh + q))
                    for q in range(2):
                        cc = 2 * hh + q
                        dve.wait_ge(ev("kn_root"), 4 * l + cc + 1)
                        chain(v.reciprocal(tA[q], tA[q]))
                        v.tensor_tensor(kk[:, q], kk[:, q], tA[q], ALU.mult).then_inc(ev("kk_ready"), 1)
                    dve.wait_ge(ev("kk_ready"), 4 * l + 2 * hh + 2)

                def rates(cc):
                    q = cc % 2
                    for nm in "rkv":
                        banks.released(dve, (nm, l, cc))
                    for d in range(2):
                        no = 8 * l + 2 * cc + d
                        banks.released(dve, ("wl", l, cc, d))
                        banks.released(dve, ("al", l, cc, d))
                        chain(v.tensor_tensor_scan(tA[2], reset, tA[0], 0.0, ALU.mult, ALU.add))
                        chain(v.tensor_tensor(tA[3], tA[2], tA[0], ALU.subtract))
                        by = lambda t: t.rearrange("p (c t) -> p c t", c=NCH)
                        ends = by(tA[2])[:, :, CH - 1]
                        chain(v.tensor_copy(wc[:, d, cc, :], ends))
                        if d == 1:
                            tot = wc[:, d, cc, :].unsqueeze(2).broadcast_to([P, NCH, CH])
                            chain(v.tensor_tensor(by(tA[0]), tot, by(tA[3]), ALU.subtract))
                            chain(v.tensor_tensor(by(tA[3]), tot, by(tA[2]), ALU.subtract))
                            chain(v.tensor_copy(tA[2], tA[0]))
                        dve.sem_inc(ev("sums_ready"), 1)
                        chain(v.tensor_tensor(tA[0], kk[:, q], tA[1], ALU.mult))
                        chain(v.tensor_scalar(tA[1], tA[1], vcol("rwkv_k_a", 4 * l + cc),
                                              col[:, K_KA1 + 4 * l + cc:K_KA1 + 4 * l + cc + 1], ALU.mult, ALU.add))
                        chain(v.tensor_tensor(tA[1], tA[1], km[:, q], ALU.mult))
                        if d == 0:
                            chain(v.tensor_copy(tA[4], tA[1]))
                        else:
                            chain(v.tensor_tensor(tA[4], tA[4], tA[1], ALU.add))
                        dve.wait_ge(ev("decays"), no + 1)
                        v.tensor_tensor(Ba[d][:, cc], Ba[d][:, cc], tA[0], ALU.mult)
                        v.tensor_tensor(Ka[d][:, cc], Ka[d][:, cc], tA[1], ALU.mult)
                        v.scalar_tensor_tensor(Za[d][:, cc], Za[d][:, cc], -1.0, kk[:, q], ALU.mult, ALU.mult)
                        v.tensor_tensor(Ra[d][:, cc, t0:NTOK], Ra[d][:, cc, t0:NTOK], rm[:, q, t0:NTOK], ALU.mult
                                        ).then_inc(ev("rates_used"), 1)
                        dve.wait_ge(ev("rates_used"), no + 1)
                    v.scalar_tensor_tensor(tA[0][:, t0:NTOK], tA[4][:, t0:NTOK], vcol("rwkv_r_k", 4 * l + cc),
                                           rm[:, q, t0:NTOK], ALU.mult, ALU.mult).then_inc(ev("bonus_in"), 1)

                def bonus(cc):
                    bank = banks.see(dve, ("bn", l, cc))
                    banks.done(v.tensor_copy(bon[:, cc, t0:NTOK], bank[:, t0:NTOK]), ("bn", l, cc))

                chain(v.memset(reset, 1.0))
                chain(v.memset(reset.rearrange("p (c t) -> p c t", c=NCH)[:, :, 0:1], 0.0))
                for hh in range(2):
                    rkv(hh)
                    for q in range(2):
                        rates(2 * hh + q)
                        bonus(2 * hh + q)
                if l > 0:
                    dve.wait_ge(ev("vf_in"), 16)
                    for cc in range(CC):
                        banks.released(dve, ("vg", l, cc))
                        chain(v.tensor_tensor(vf[:, cc], vf[:, cc], vT[:, cc], ALU.subtract))
                        chain(v.tensor_tensor(vf[:, cc], vf[:, cc], tA[cc], ALU.mult))
                        chain(v.tensor_tensor(vT[:, cc], vT[:, cc], vf[:, cc], ALU.add))
                for cc in range(CC):
                    banks.released(dve, ("bn", l, cc))
                    chain(v.tensor_tensor(bon[:, cc, t0:NTOK], bon[:, cc, t0:NTOK], vT[:, cc, t0:NTOK], ALU.mult))
                rot = rm[:, 0, 0:LAT]
                for nm, dst in (("aq", qT), ("ak", kT)):
                    for cc in range(CC):
                        bank = banks.see(dve, ("rope", l, nm, cc))
                        banks.done(v.tensor_tensor(rot, bank[:, 0:LAT], sin, ALU.mult), ("rope", l, nm, cc))
                        banks.released(dve, ("rope", l, nm, cc))
                        z = dst[:, cc, CTX:NTOK]
                        chain(v.tensor_tensor(z, z, cos, ALU.mult))
                        chain(v.tensor_tensor(z, z, rot, ALU.add))
                        dve.sem_inc(ev("roped"), 1)

            def attention(l):
                units = [(s, h, qt) for s in streams(l) for h in range(CC) for qt in range(2)]

                def maxima(n):
                    nk = CTX if units[n][0] == 0 else NTOK
                    st = stat[:, n % 2, :]
                    for m in range(2):
                        bank = banks.see(dve, ("s", l, n, m))
                        chain(v.reduce_max(st[:, m:m + 1], bank[:, 0:nk], AX.X))
                    v.tensor_scalar(st[:, 2:4], st[:, 0:2], -(QK ** -0.5), None, ALU.mult
                                    ).then_inc(ev("max_ready"), 1)

                def weights(n):
                    nk = CTX if units[n][0] == 0 else NTOK
                    st = stat[:, n % 2, :]
                    for m in range(2):
                        banks.released(dve, ("s", l, n, m))
                    chain(v.reciprocal(st[:, 6:8], st[:, 4:6]))
                    chain(v.tensor_tensor(st[:, 7:8], st[:, 7:8], col[:, K_NLAM + l:K_NLAM + l + 1], ALU.mult))
                    if n >= 2:
                        banks.see(dve, ("wt", l, n - 2))
                    w = Wm[n % 2][:, 0:nk]
                    chain(v.tensor_scalar(w, Pm[n % 2][0][:, 0:nk], st[:, 6:7], None, ALU.mult))
                    v.scalar_tensor_tensor(w, Pm[n % 2][1][:, 0:nk], st[:, 7:8], w, ALU.mult, ALU.add
                                           ).then_inc(ev("w_ready"), 1)

                for n in range(len(units) + 1):
                    if n < len(units):
                        maxima(n)
                    if n > 0:
                        weights(n - 1)
                t0 = first(l)
                for h in range(CC):
                    banks.released(dve, ("on", l, h))
                    chain(v.reciprocal(asq[h][:, t0:NTOK], asq[h][:, t0:NTOK]))
                    z = hT[:, h, t0:NTOK]
                    chain(v.scalar_tensor_tensor(z, z, col[:, K_SUBG + l:K_SUBG + l + 1], asq[h][:, t0:NTOK],
                                                 ALU.mult, ALU.mult))
                    dve.sem_inc(ev("att_normed"), 1)
                for d in range(2):
                    z = at(A_S + d * len(names) * 512, 5 * 512)
                    chain(v.memset(z, 0.0))
                    chain(v.memset(bd[d]["S"], 0.0))
                chain(v.memset(hT[:, 4:8, t0:NTOK], 0.0))
                dve.sem_inc(ev("cleared"), 1)

            def chunks(l, s):
                with_y, lc = loops[l, s]
                idb = ident.unsqueeze(1).broadcast_to([P, CC, P])
                left = dve.alloc_register(f"left_dve{l}{s}")
                dve.reg_mov(left, NCH // 2 - 1)
                with dve.Fori(0, NCH // 2) as i:
                    back = dve.snap(left, min_val=0, max_val=NCH // 2 - 1)
                    for nme in lc["dve", 0].names:
                        for d in range(2):
                            t, own, pe_c = bd[d], lc["dve", d], lc["pe", d]
                            chunk = (i if d == 0 else back) + 4 * s

                            def bank(product):
                                dve.wait_ge(pe_c.sem, pe_c.after(i, product))
                                b = psum[4 * d + pe_c.names.index(product) % 4]
                                return b.rearrange("p (a b) -> p a b", a=CC)
                            if nme == "NTs":
                                ins = v.tensor_tensor(t["NT"], bank("NT"), mask(d, 0), ALU.mult)
                            elif nme == "XTm":
                                ins = v.tensor_tensor(t["XT"], bank("NT"), mask(d, 2), ALU.mult)
                            elif nme == "Xm":
                                ins = v.tensor_tensor(t["X"], bank("N"), mask(1 - d, 2), ALU.mult)
                            elif nme in ("XTi", "Xi"):
                                dve.wait_ge(own.sem, own.after(i, nme[:-1] + "m"))
                                z = t[nme[:-1]]
                                ins = v.tensor_tensor(z, z, idb, ALU.add)
                            elif nme == "AZ":
                                ins = v.tensor_tensor(t["AZ"], bank("AZ"), mask(d, 0), ALU.mult)
                            elif nme in ("AB", "AK"):
                                ins = v.tensor_tensor(t[nme], bank(nme), mask(d, 1), ALU.mult)
                            elif nme[0] == "T":
                                ins = v.tensor_tensor(t["T1"], bank(nme), idb, ALU.add)
                            elif nme[0] == "Y":
                                h = int(nme[1])
                                r = slice(64 * h, 64 * h + 64)
                                y = hT[r, 4:8, bass.ds(chunk * CH, CH)]
                                ins = v.tensor_tensor(y, y, bank("Y")[r, :, 64 * h:64 * h + 64], ALU.add)
                            elif nme == "ST1":
                                ins = v.tensor_tensor(t["S"], t["S"], bank("ST"), ALU.add)
                            elif nme == "ST2":
                                dve.wait_ge(own.sem, own.after(i, "ST1"))
                                w = wc[:, d, :, bass.ds(chunk, 1)].broadcast_to([P, CC, P])
                                ins = v.tensor_tensor(t["S"], t["S"], w, ALU.mult)
                            ins.then_inc(own.sem, 1)
                    dve.reg_sub(left, left, 1)

            def finish(l):
                t0 = first(l)
                for cc in range(CC):
                    z = hT[:, 4 + cc, t0:NTOK]
                    bank = banks.see(dve, ("ym", l, cc))
                    banks.done(v.scalar_tensor_tensor(z, bank[:, t0:NTOK], -1.0 / CH, z, ALU.mult, ALU.add),
                               ("ym", l, cc))
                for cc in range(CC):
                    z = hT[:, 4 + cc, t0:NTOK]
                    banks.released(dve, ("yv", l, cc))
                    inv = fin[cc][:, t0:NTOK]
                    chain(v.reciprocal(inv, inv))
                    chain(v.scalar_tensor_tensor(z, z, vcol("lnx_w", 4 * l + cc), inv, ALU.mult, ALU.mult))
                    chain(v.scalar_tensor_tensor(z, z, vcol("lnx_b", 4 * l + cc), bon[:, cc, t0:NTOK], ALU.add,
                                                 ALU.add))
                    bank = banks.see(dve, ("yg", l, cc))
                    banks.done(v.tensor_tensor(z, z, bank[:, t0:NTOK], ALU.mult), ("yg", l, cc))

            def add_gated(keys, l, g):
                for c in range(DC):
                    bank = banks.see(dve, keys(c))
                    for s in streams(l):
                        r = slice(s * CTX, (s + 1) * CTX)
                        ins = v.scalar_tensor_tensor(xT[:, c, r], bank[:, r], mod[:, l, g + c, s:s + 1], xT[:, c, r],
                                                     ALU.mult, ALU.add)
                    banks.done(ins, keys(c))

            def w_out(l):
                dve.wait_ge(ev("x_back"), 16 * (l + 1))
                add_gated(lambda c: ("wo", l, c), l, 16)

            def feed_forward():
                for c in range(FC):
                    bank = banks.see(dve, ("w1", c))
                    dve.wait_ge(ev("ff_sig"), c + 1)
                    banks.done(v.tensor_tensor(ff[:, c, :], ffs[c % 2], bank, ALU.mult), ("w1", c))
                    bank = banks.see(dve, ("w3", c))
                    banks.released(dve, ("w1", c))
                    banks.done(v.tensor_tensor(ff[:, c, :], ff[:, c, :], bank, ALU.mult), ("w3", c))
                add_gated(lambda c: ("f2", c), 0, 40)

            def route():
                big = 1000.0

                def w8(t, k, n=8):
                    return rt[:, t, k:k + n]

                for t in range(2):
                    bank = banks.see(dve, ("lg", t))
                    banks.done(v.tensor_copy(w8(t, LG), bank[:, 0:8]), ("lg", t))
                    banks.released(dve, ("lg", t))
                for t in range(2):
                    chain(v.max(w8(t, MX), w8(t, LG)))
                    chain(v.memset(w8(t, R5), 1.0))
                    chain(v.tensor_scalar(w8(t, R1), w8(t, LG), w8(t, MX, 1), None, ALU.is_equal))
                    chain(v.tensor_tensor_scan(w8(t, R2), w8(t, R5), w8(t, R1), 0.0, ALU.mult, ALU.add))
                    chain(v.scalar_tensor_tensor(w8(t, R1), w8(t, R2), 1.0, w8(t, R1), ALU.is_equal, ALU.mult))
                    chain(v.tensor_scalar(w8(t, R4), w8(t, R1), -1.0, 1.0, ALU.mult, ALU.add))
                    chain(v.scalar_tensor_tensor(w8(t, R3), w8(t, LG), w8(t, MX + 1, 1), w8(t, R4), ALU.is_equal,
                                                 ALU.mult))
                    chain(v.tensor_tensor_scan(w8(t, R2), w8(t, R5), w8(t, R3), 0.0, ALU.mult, ALU.add))
                    chain(v.scalar_tensor_tensor(w8(t, R3), w8(t, R2), 1.0, w8(t, R3), ALU.is_equal, ALU.mult))
                    chain(v.tensor_tensor(w8(t, CHO), w8(t, R1), w8(t, R3), ALU.add))
                    dve.sem_inc(ev("chosen"), 1)
                    chain(v.tensor_tensor(w8(t, SC, 1), w8(t, MX + 1, 1), w8(t, MX, 1), ALU.subtract))
                dve.sem_inc(ev("gate_in"), 1)
                dve.wait_ge(ev("gate_exp"), 1)
                for t in range(2):
                    chain(v.tensor_scalar(w8(t, SC + 2, 1), w8(t, SC + 1, 1), 1.0, None, ALU.add))
                    chain(v.reciprocal(w8(t, SC + 3, 1), w8(t, SC + 2, 1)))
                    chain(v.tensor_tensor(w8(t, SC + 4, 1), w8(t, SC + 1, 1), w8(t, SC + 3, 1), ALU.mult))
                    chain(v.tensor_scalar(w8(t, R3), w8(t, R3), w8(t, SC + 4, 1), None, ALU.mult))
                    chain(v.scalar_tensor_tensor(w8(t, CI), w8(t, R1), w8(t, SC + 3, 1), w8(t, R3), ALU.mult,
                                                 ALU.add))
                    bank = banks.see(dve, ("rk", t))
                    chain(v.scalar_tensor_tensor(w8(t, RI), bank[:, 0:8], big, w8(t, CHO), ALU.add, ALU.mult))
                    banks.done(v.tensor_scalar(w8(t, RI), w8(t, RI), -big, None, ALU.add), ("rk", t))
                    banks.released(dve, ("rk", t))
                bank = banks.see(dve, ("ct", 0))
                t1, t2, t3, t4, one = w8(0, R1), w8(0, R2), w8(0, R3), w8(0, R4), w8(0, R5)
                banks.done(v.tensor_scalar(t1, bank[:, 0:8], float(SLOTS), None, ALU.is_gt), ("ct", 0))
                banks.released(dve, ("ct", 0))
                chain(v.tensor_tensor_scan(t2, one, t1, 0.0, ALU.mult, ALU.add))
                ids = w8(1, R1, 16)
                chain(v.memset(ids, 0.0))
                chain(v.tensor_copy(ids[:, 0:8], iota[:, 0:8]))
                chain(v.tensor_scalar(ids[:, 15:16], t2[:, 7:8], float(N_EXP), None, ALU.add))
                for r in range(MAX_ITEMS - N_EXP):
                    chain(v.scalar_tensor_tensor(t3, t2, float(r + 1), t1, ALU.is_equal, ALU.mult))
                    chain(v.tensor_tensor_reduce(t4, t3, iota[:, 0:8], 1.0, 0.0, ALU.mult, ALU.add,
                                                 ids[:, 8 + r:9 + r]))
                    for t in range(2):
                        z = w8(t, RI + 8 + r, 1)
                        chain(v.tensor_scalar(w8(1, R4), w8(t, RI), 2 * big - SLOTS, None, ALU.add))
                        chain(v.tensor_tensor_reduce(t4, t3, w8(1, R4), 1.0, 0.0, ALU.mult, ALU.add, z))
                        chain(v.tensor_scalar(z, z, -2 * big, None, ALU.add))
                        chain(v.tensor_tensor_reduce(t4, t3, w8(t, CI), 1.0, 0.0, ALU.mult, ALU.add,
                                                     w8(t, CI + 8 + r, 1)))
                chain(v.tensor_copy(idx[:, :], ids))
                dve.sem_inc(ev("items_ready"), 1)

            def experts():
                T = dve.value_load(idx[0:1, 15:16], min_val=N_EXP, max_val=MAX_ITEMS)
                own, pe_c, act_c = item_cnt["dve"], item_cnt["pe"], item_cnt["act"]
                with dve.Fori(0, T) as i:
                    def bank(nme):
                        dve.wait_ge(pe_c.sem, pe_c.after(i, nme))
                        return psum[item_banks.index(nme) % 8]

                    def step(ins):
                        ins.then_inc(own.sem, 1)

                    for t in range(2):
                        step(v.tensor_scalar(Pe[:, t, :], iota, rt[:, t, bass.ds(i + RI, 1)], None, ALU.is_equal))
                    for t in range(2):
                        step(v.tensor_scalar(Pw[:, t, :], iota, rt[:, t, bass.ds(i + RI, 1)],
                                             rt[:, t, bass.ds(i + CI, 1)], ALU.is_equal, ALU.mult))
                    for f in range(7):
                        z = u[:, f * 512:(f + 1) * 512]
                        dve.wait_ge(act_c.sem, act_c.after(i, f"S{f}"))
                        step(v.tensor_tensor(z, z, bank(f"A{f}"), ALU.mult))
                        dve.wait_ge(own.sem, own.after(i, f"UA{f}"))
                        step(v.tensor_tensor(z, z, bank(f"B{f}"), ALU.mult))
                    for g in range(4):
                        b = bank(f"C{g}")
                        for q in range(2):
                            c = 2 * g + q
                            z = xT[:, c, CTX:NTOK]
                            step(v.scalar_tensor_tensor(z, b[:, q * 256:(q + 1) * 256], mod[:, 1, 40 + c, 1:2], z,
                                                        ALU.mult, ALU.add))
                dve.wait_ge(own.sem, T * own.per + own.base)
                dve.sem_inc(ev("items_done"), 1)

            def final():
                for t in range(2):
                    for half in range(2):
                        bank = banks.see(dve, ("fin", t, half))
                        banks.done(v.tensor_copy(out_tile[:, t, half * 512:(half + 1) * 512], bank),
                                   ("fin", t, half))

            seq = [setup]
            for l in range(DEPTH):
                seq += [lambda l=l: norm((l, 0), 0, srt, rst), lambda l=l: project(l), lambda l=l: attention(l),
                        lambda l=l: chunks(l, 0), lambda l=l: chunks(l, 1), lambda l=l: finish(l),
                        lambda l=l: w_out(l)]
                if l == 0:
                    seq += [lambda: norm((0, 1), 0, srt, rst), feed_forward]
                else:
                    seq += [lambda: norm((1, 1), CTX, rsm[:, 0], rsm[:, 1]), route, experts]
            seq += [lambda: norm((2, 0), CTX, rsm[:, 0], rsm[:, 1]), final]
            for f in seq[:LAST]:
                f()

        @block.gpsimd
        def _(pool):
            g = nc.gpsimd
            for d in range(2):
                pool.sem_inc(ev(f"chunk_pool{d}"), PRIME)

            def chunks(l, s):
                with_y, lc = loops[l, s]
                if s == 0:
                    pool.wait_ge(ev("cleared"), l + 1)
                for d in range(2):
                    pool.wait_ge(lc["pe", d].sem, lc["pe", d].before(0))
                last_use = {"B": "AB" if with_y else "BT", "K": "AK" if with_y else "KT", "V": "VT", "Z": "RHS",
                            "R": "Y"}
                arrays = {"Z": Za, "R": Ra, "B": Ba, "K": Ka, "V": [vT, vT]}
                left = pool.alloc_register(f"left_pool{l}{s}")
                pool.reg_mov(left, NCH // 2 - 1)
                with pool.Fori(0, NCH // 2) as i:
                    back = pool.snap(left, min_val=0, max_val=NCH // 2 - 1)
                    for nme in lc["pool", 0].names:
                        for d in range(2):
                            t, own, pe_c, dve_c = bd[d], lc["pool", d], lc["pe", d], lc["dve", d]
                            if (nme, d) == (own.names[0], 0):
                                pool.wait_ge(lc["pool", 1].sem, lc["pool", 1].before(i))
                            elif d == 0:
                                pool.wait_ge(lc["pool", 1].sem, lc["pool", 1].after(i, before))
                            else:
                                pool.wait_ge(lc["pool", 0].sem, lc["pool", 0].after(i, nme))
                            if nme[0] == "L":
                                a, h = nme[1], int(nme[2])
                                pool.wait_ge(pe_c.sem, pe_c.in_last(i, last_use[a]))
                                tok = ((i if d == 0 else back) + 4 * s) * CH
                                r = slice(64 * h, 64 * h + 64)
                                ins = g.tensor_copy(t[a][r, :, 64 * h:64 * h + 64],
                                                    arrays[a][d][r, :, bass.ds(tok, CH)])
                            else:
                                b = int(nme[1:])
                                pool.wait_ge(dve_c.sem, dve_c.after(i, "NTs"))
                                if b > 1:
                                    pool.wait_ge(pe_c.sem, pe_c.after(i, f"T{b - 1}"))
                                ins = g.tensor_tensor(t["MT"], t["NT"], mask(d, 2 + b), ALU.mult)
                            ins.then_inc(own.sem, 1)
                        before = nme
                    pool.reg_sub(left, left, 1)

            nop = lambda: None
            seq = [nop]
            for l in range(DEPTH):
                seq += [nop, nop, nop, lambda l=l: chunks(l, 0), lambda l=l: chunks(l, 1), nop, nop]
                seq += [nop, nop] if l == 0 else [nop, nop, nop]
            for f in seq[:LAST]:
                f()

        @block.sync
        def _(sp):
            def ring_load(n):
                key, src, nk, nn = loads[n]
                if n >= RING:
                    free_slot(sp, used_by[loads[n - RING][0]])
                sp.dma_start(ring_view(n), src).then_inc(ring_full[n % RING], 16)

            def free_slot(eng, use):
                if isinstance(use, tuple):
                    banks.see(eng, use)
                else:
                    eng.wait_ge(ev("w2_part"), use)

            done = [0]

            def load_until(key):
                n = load_at[key]
                while done[0] <= n:
                    ring_load(done[0])
                    done[0] += 1

            def setup():
                load_until(("ada", DEPTH - 1, 23))

            def project(l):
                if l == 0:
                    banks.see(sp, ("mod", DEPTH - 1))
                else:
                    banks.see(sp, ("yg", 0, CC - 1))
                    for d in range(2):
                        c_ = loops[0, 1][1]["pe", d]
                        sp.wait_ge(c_.sem, c_.end(NCH // 2))
                ws = [(lw2[0:64, :], inp["rwkv_w2"][l].rearrange("a j n -> (a j) n")),
                      (la2[0:64, :], inp["rwkv_a2"][l].rearrange("a j n -> (a j) n")),
                      (g2[0:96, :], inp["rwkv_g2"][l])]
                if l:
                    ws += [(lv1, inp["rwkv_v1"][0].rearrange("(k p) n -> p k n", p=P)),
                           (lv2[0:32, :], inp["rwkv_v2"][0])]
                for dst, src in ws:
                    sp.dma_start(dst, src).then_inc(ev("lora_w_in"), 16)
                load_until(("av1", l))

            def w_out(l):
                load_until(("wout", l, 3))

            def feed_forward():
                load_until(("w2", 3, 2))

            def route():
                banks.released(sp, ("yg", 1, CC - 1))
                sp.wait_ge(ev("h_ready"), norm_no[1, 1] + 1)
                sp.dma_start(rw, inp["router_w"][0].rearrange("(k p) n -> p k n", p=P)
                             ).then_inc(ev("router_in"), 16)

            def experts():
                sp.wait_ge(ev("items_ready"), 1)
                T = sp.value_load(idx[0:1, 15:16], min_val=N_EXP, max_val=MAX_ITEMS)
                pe_c = item_cnt["pe"]
                reader = [x for f in range(7) for x in (f"A{f}", f"B{f}")] + [f"D{m}" for m in range(6)] + ["Y1"]
                with sp.Fori(0, T) as i:
                    e = sp.value_load(idx[0:1, bass.ds(i, 1)], min_val=0, max_val=N_EXP - 1)
                    for m in range(21):
                        if m < RING2:
                            sp.wait_ge(pe_c.sem, pe_c.in_last(i, reader[m + 21 - RING2]))
                        else:
                            sp.wait_ge(pe_c.sem, pe_c.after(i, reader[m - RING2]))
                        dst = at(A_RING2 + (m % RING2) * SLOT2, SLOT2)
                        if m < 14:
                            w = inp["exp_w1" if m % 2 == 0 else "exp_w3"]
                            src = w[0, bass.ds(e, 1), :, (m // 2) * 512:(m // 2 + 1) * 512].rearrange(
                                "e (k p) n -> p (e k) n", p=P)
                            dst = dst.rearrange("p (k n) -> p k n", k=DC)
                        else:
                            src = inp["exp_w2"][0, bass.ds(e, 1), (m - 14) * 512:(m - 13) * 512, :].rearrange(
                                "e (k p) n -> p (e k) n", p=P)
                            dst = dst.rearrange("p (k n) -> p k n", k=4)
                        sp.dma_start(dst, src).then_inc(ev(f"ring2_full{m % RING2}"), 16)

            def final():
                for t in range(2):
                    for half in range(2):
                        banks.released(sp, ("fin", t, half))
                    sp.dma_start(out[0, t * P:(t + 1) * P, :], out_tile[:, t, :]).then_inc(ev("out_written"), 16)
                sp.wait_ge(ev("out_written"), 32)

            nop = lambda: None
            seq = [setup]
            for l in range(DEPTH):
                seq += [nop, lambda l=l: project(l), nop, nop, nop, nop, lambda l=l: w_out(l)]
                seq += [nop, feed_forward] if l == 0 else [nop, route, experts]
            seq += [nop, final]
            for f in seq[:LAST]:
                f()
            if LAST > 1:
                sp.wait_ge(ev("x_parked"), 16 * (2 if LAST > 10 else 1))
            if LAST > 2:
                sp.wait_ge(ev("vf_out"), 16)


_INS = ["x", "c", "ctx", "c_ctx", "ada_w", "ada_b", "norm1_g", "norm2_g", "w_in", "w_out", "diff_lambda", "subln_g",
        "rwkv_mu", "rwkv_w0", "rwkv_w2", "rwkv_a0", "rwkv_a2", "rwkv_v0", "rwkv_v1", "rwkv_v2", "rwkv_g2",
        "rwkv_k_k", "rwkv_k_a", "rwkv_r_k", "lnx_w", "lnx_b", "ffn_w1", "ffn_w3", "ffn_w2", "router_w", "exp_w1",
        "exp_w3", "exp_w2", "final_g"]


def kernel(**inputs):
    import concourse.bacc as _bacc
    from concourse.bass_utils import run_bass_kernel_spmd as _run

    nc = _bacc.Bacc("TRN2", target_bir_lowering=False, num_devices=1)
    arrays, aps = {}, {}
    for name in _INS:
        a = np.ascontiguousarray(inputs[name])
        arrays[f"in_{name}"] = a
        aps[name] = nc.dram_tensor(f"in_{name}", a.shape, mybir.dt.from_np(a.dtype), kind="ExternalInput").ap()
    tables = constant_tables()
    arrays["in_const_tables"] = tables
    aps["const_tables"] = nc.dram_tensor("in_const_tables", tables.shape, F32, kind="ExternalInput").ap()
    out = nc.dram_tensor("out_0", (1, LAT, D), F32, kind="ExternalOutput").ap()
    vf_dram = nc.dram_tensor("first_values", (P, CC * NTOK), F32).ap()
    x_dram = nc.dram_tensor("parked_x", (P, DC * NTOK), F32).ap()
    hybrid_backbone(nc, aps, out, vf_dram, x_dram)
    r = _run(nc, [arrays], core_ids=[0])
    return r.results[0]["out_0"]
```

```python
from contextlib import ExitStack
import math

import numpy as np
import concourse.bass as bass
from concourse import mybir

F32 = mybir.dt.float32
F32R = mybir.dt.float32r
I32 = mybir.dt.int32
ALU = mybir.AluOpType
ACT = mybir.ActivationFunctionType
AX = mybir.AxisListType

P = 128
D = 1024
DC = D // P
CTX, LAT = 256, 256
NTOK = CTX + LAT
DEPTH = 2
HALF = 512
CC = HALF // P
QK = 64
N_IN = 3296
LORA_COLS = 224
D_FF = 2816
FC = D_FF // P
N_EXP = 8
D_FFE = 3584
GRID_W = 64
CH = 64
NCH = NTOK // CH
LEVELS = 6
DECAY = math.exp(-0.5)
NORM_EPS, SUBLN_EPS, LNX_EPS = 1e-6, 1e-5, 64e-5
SLOTS = 128
MAX_ITEMS = N_EXP + (2 * LAT) // (SLOTS + 1)

C_IDENT, C_ONES, C_ONESBD, C_PERM, C_UPPER, C_IOTA = (k * P for k in range(6))
C_MASK = 6 * P
N_MASK = 2 + LEVELS
C_COS = C_MASK + 2 * N_MASK * P
C_SIN = C_COS + LAT
N_CONST = C_SIN + LAT


def constant_tables():
    t = np.zeros((P, N_CONST), np.float32)
    i = np.arange(P)
    t[:, C_IDENT:C_IDENT + P] = np.eye(P)
    t[:, C_ONES:C_ONES + P] = 1.0
    same = (i[:, None] // CH) == (i[None, :] // CH)
    t[:, C_ONESBD:C_ONESBD + P] = same
    t[:, C_PERM:C_PERM + P] = (i[:, None] ^ 16) == i[None, :]
    t[:, C_UPPER:C_UPPER + P] = i[:, None] < i[None, :]
    t[:, C_IOTA:C_IOTA + P] = i[None, :]
    s, q = i[:, None] % CH, i[None, :] % CH
    for d in range(2):
        a, b = (s, q) if d == 0 else (q, s)
        m = [a < b, a <= b] + [(a // (2 * w) == b // (2 * w)) & (a % (2 * w) < w) & (b % (2 * w) >= w)
                               for w in (2 ** k for k in range(LEVELS))]
        for k, v in enumerate(m):
            at = C_MASK + (d * N_MASK + k) * P
            t[:, at:at + P] = v & same
    tok = np.arange(LAT)
    inv = (10000.0 ** (-np.arange(0, 32, 2, dtype=np.float32) / 32)).astype(np.float32)
    dim = i % 64
    pos = np.where((dim < 32)[:, None], (tok // GRID_W)[None, :], (tok % GRID_W)[None, :]).astype(np.float32)
    ang = pos * inv[dim % 16][:, None]
    t[:, C_COS:C_COS + LAT] = np.cos(ang)
    t[:, C_SIN:C_SIN + LAT] = np.sin(ang) * np.where(dim % 32 < 16, -1.0, 1.0)[:, None]
    return t


VEC_A = [("ada_b", 96)]
VEC_B = [("norm1_g", 16), ("norm2_g", 16), ("final_g", 8), ("rwkv_w0", 16), ("rwkv_a0", 16), ("rwkv_k_k", 8),
         ("rwkv_k_a", 8), ("rwkv_r_k", 8), ("lnx_w", 8), ("lnx_b", 8), ("rwkv_v0", 4)]
VEC_C = [("rwkv_mu", 48), ("subln_g", 2), ("c", 8), ("c_ctx", 8)]
VEC_TILES = [VEC_A, VEC_B, VEC_C]


def vector_columns():
    cols, at, tiles = {}, 0, []
    for rows in VEC_TILES:
        first = at
        for name, n in rows:
            cols[name] = at
            at += n
        tiles.append((first, at - first))
    return cols, tiles, at


A_CONST = 0
A_VEC = N_CONST
A_MOD = A_VEC + 278
A_GAIN = A_MOD + DEPTH * 96
A_COL = A_GAIN + DEPTH * 32
A_H = 4000
A_X = A_H + 4096
A_Z = A_X
A_V = A_Z + 16384
A_BON = A_V + 2048
A_SG = A_BON + 2048
A_S = A_SG + 1024
A_RING = A_S + 17408
RING, SLOT = 3, 2048
ARENA = A_RING + RING * SLOT
A_RING2 = A_X + 4096
RING2, SLOT2 = 6, SLOT
PARTS = 3
A_HTOK = A_RING2 + RING2 * SLOT2
TILES = 42
A_TAIL = A_BON
assert A_HTOK + 2 * D <= A_TAIL
PRIME = 128

(K_LAM, K_NLAM, K_SUBG, K_MU1, K_KA1, K_EPS, K_WC, K_CS, K_SMALL) = (
    0, 2, 4, 6, 30, 38, 42, 106, 122)
SEQ_END = 138
assert A_COL + SEQ_END <= A_H, (A_COL + SEQ_END, A_H)


class Banks:

    def __init__(self, psum, full, free):
        self.psum, self.full, self.free = psum, full, free
        self.uses, self.where, self.turn = [0] * 8, {}, 0

    def take(self, pe, key):
        b = self.turn % 8
        self.turn += 1
        if self.uses[b]:
            pe.wait_ge(self.free[b], self.uses[b])
        self.uses[b] += 1
        self.where[key] = (b, self.uses[b])
        return self.psum[b]

    def fill(self, ins, key):
        ins.then_inc(self.full[self.where[key][0]], 1)

    def see(self, eng, key):
        b, n = self.where[key]
        eng.wait_ge(self.full[b], n)
        return self.psum[b]

    def done(self, ins, key):
        ins.then_inc(self.free[self.where[key][0]], 1)

    def released(self, eng, key):
        b, n = self.where[key]
        eng.wait_ge(self.free[b], n)

    def all_free(self, pe):
        for b in range(8):
            if self.uses[b]:
                pe.wait_ge(self.free[b], self.uses[b])


class Chain:

    def __init__(self, eng, sem):
        self.eng, self.sem, self.n = eng, sem, 0

    def __call__(self, ins):
        ins.then_inc(self.sem, 1)
        self.n += 1
        self.eng.wait_ge(self.sem, self.n)
        return ins


class LoopCount:

    def __init__(self, sem, base, names):
        self.sem, self.base, self.names = sem, base, list(names)
        self.per = len(self.names)

    def after(self, i, name):
        return i * self.per + (self.base + self.names.index(name) + 1)

    def before(self, i):
        return i * self.per + self.base

    def in_last(self, i, name):
        return i * self.per + (self.base - self.per + self.names.index(name) + 1)

    def end(self, n):
        return self.base + n * self.per


def loop_lists(with_y, s):
    lv = range(1, LEVELS)
    pe = ["NT", "N", "AZ", "BT", "KT", "VT"] + (["AB", "AK"] if with_y else [])
    for b in lv:
        pe += [f"T{b}"] + ([f"X{b}"] if b < LEVELS - 1 else []) + [f"XT{b}"]
    pe += ["RHS", "U"] + (["Y"] if with_y else []) + ["ST"]
    dve = ["NTs", "XTm", "Xm", "XTi", "Xi", "AZ"] + (["AB", "AK"] if with_y else [])
    dve += [f"T{b}" for b in lv] + (["AN"] if s == 0 else []) + (["Y0", "Y1"] if with_y else []) + ["ST1", "ST2"]
    act = ["BT", "KT", "VT"]
    for b in lv:
        act += ([f"X{b}"] if b < LEVELS - 1 else []) + [f"XT{b}"]
    act += ["RHS", "U"]
    pool = ["LB0", "LB1", "LK0", "LK1", "LV0", "LV1", "LZ0", "LZ1"] + (["LR0", "LR1"] if with_y else [])
    pool += [f"M{b}" for b in lv]
    return pe, dve, act, pool


def hybrid_backbone(nc, inp, out, vf_dram, x_dram, stages=99, dump=None):
    ctx = ExitStack()
    with ctx:
        front = ctx.enter_context(nc.sbuf_tensor("front", [P, A_TAIL], F32))
        with nc.sbuf_tensor("tail", [P, ARENA - A_TAIL], F32) as tail:
            pass
        wparts = ctx.enter_context(nc.sbuf_tensor("weight_parts", [P, 2 * PARTS, SLOT2], F32R))
        tparts = ctx.enter_context(nc.sbuf_tensor("token_parts", [P, 2, (DC + D_FFE // P) * SLOTS], F32R))
        ye_ = ctx.enter_context(nc.sbuf_tensor("expert_out", [P, D], F32))
        idx = ctx.enter_context(nc.sbuf_tensor("idx", [P, 16], I32))
        psum = [ctx.enter_context(nc.psum_tensor(f"ps{b}", [P, 512], F32))[:, :] for b in range(8)]
        named = {}

        def ev(name):
            if name not in named:
                named[name] = ctx.enter_context(nc.semaphore(name))
            return named[name]

        def at(off, *dims):
            n = int(np.prod(dims))
            assert off + n <= A_TAIL or off >= A_TAIL
            v = front[:, off:off + n] if off < A_TAIL else tail[:, off - A_TAIL:off - A_TAIL + n]
            if len(dims) == 2:
                v = v.rearrange("p (a b) -> p a b", a=dims[0])
            if len(dims) == 3:
                v = v.rearrange("p (a b c) -> p a b c", a=dims[0], b=dims[1])
            return v

        banks = Banks(psum, [ev(f"bank_full{b}") for b in range(8)], [ev(f"bank_free{b}") for b in range(8)])
        ring_full = [ev(f"ring_full{k}") for k in range(RING)]

        cols, vec_tiles, n_vec = vector_columns()
        ident, ones, onesbd = at(C_IDENT, P), at(C_ONES, P), at(C_ONESBD, P)
        perm, upper, iota = at(C_PERM, P), at(C_UPPER, P), at(C_IOTA, P)
        masks = at(C_MASK, 2 * N_MASK, P)
        cos, sin = at(C_COS, LAT), at(C_SIN, LAT)
        vec = at(A_VEC, n_vec)
        mod = at(A_MOD, DEPTH, 48, 2)
        gain = at(A_GAIN, DEPTH * 2, DC, 2)
        col = at(A_COL, SEQ_END)
        cs = at(A_COL + K_CS, DC, 2)
        wc = at(A_COL + K_WC, 2, CC, NCH)
        epsc = {NORM_EPS: col[:, K_EPS:K_EPS + 1], SUBLN_EPS: col[:, K_EPS + 1:K_EPS + 2],
                LNX_EPS: col[:, K_EPS + 2:K_EPS + 3]}
        hT = at(A_H, DC, NTOK)
        xT = at(A_X, DC, NTOK)

        def vcol(name, k):
            return vec[:, cols[name] + k:cols[name] + k + 1]

        def mask(d, k):
            return masks[:, d * N_MASK + k:d * N_MASK + k + 1, :].broadcast_to([P, CC, P])

        def first(l):
            return 0 if l < DEPTH - 1 else CTX

        def streams(l):
            return [0, 1] if l < DEPTH - 1 else [1]

        modrow = at(A_X + 4096, DEPTH, 24 * 256)
        vec_rows = [at(A_V + k * P, P) for k in range(3)]
        lamrow = at(A_V + 512, DEPTH, 4, QK)
        lamtmp = at(A_V + 1024, QK)
        xin = at(A_H, 4, D)
        sq = at(A_S, 4, NTOK)
        srt = at(A_S + 2048, NTOK)
        rst = at(A_S + 2560, NTOK)
        qT, kT, vtok = at(A_S, CC, NTOK), at(A_S + 2048, CC, NTOK), at(A_S + 4096, 4, HALF)
        A_T = A_S + 6144
        rm, km = at(A_T, 2, NTOK), at(A_T + 1024, 2, NTOK)
        th, ad = at(A_T + 2048, NTOK), at(A_T + 2560, NTOK)
        lw2, la2, lv2 = at(A_T + 3072, HALF), at(A_T + 3584, HALF), at(A_T + 4096, HALF)
        lv1 = at(A_T + 4608, CC, 32)
        reset = at(A_T + 4736, NTOK)
        kk = at(A_T + 5248, 2, NTOK)
        tA = [at(A_T + 6272 + k * NTOK, NTOK) for k in range(5)]
        vf = at(A_T + 8832, CC, NTOK)
        assert A_T + 8832 + 2048 <= A_RING
        sgd, g2 = at(A_SG, NTOK), at(A_SG + 512, HALF)
        vT = at(A_V, CC, NTOK)
        bon = at(A_BON, CC, NTOK)
        Za = [at(A_Z + (0 + d) * 2048, CC, NTOK) for d in range(2)]
        Ra = [at(A_Z + (2 + d) * 2048, CC, NTOK) for d in range(2)]
        Ba = [at(A_Z + (4 + d) * 2048, CC, NTOK) for d in range(2)]
        Ka = [at(A_Z + (6 + d) * 2048, CC, NTOK) for d in range(2)]
        Pm = [[at(A_T + (2 * b + m) * 512, 512) for m in range(2)] for b in range(2)]
        Wm = [at(A_T + 2048 + b * 512, 512) for b in range(2)]
        WT = [at(A_T + 3072 + b * 1024, 4, 256) for b in range(2)]
        stat = at(A_COL + K_SMALL, 2, 8)
        own, kept = ["NT", "MT", "AZ", "AB", "AK", "X", "XT", "T1", "BT", "KT", "VT"], ["Z", "R", "B", "K", "V", "S"]
        A_KEPT = A_S + 2 * len(own) * 512
        assert A_KEPT >= A_T + 5120 and A_KEPT + 2 * len(kept) * 512 <= A_RING
        bd = [{n: at(A_S + (d * len(own) + k) * 512, CC, P) for k, n in enumerate(own)} for d in range(2)]
        for d in range(2):
            bd[d].update({n: at(A_KEPT + (d * len(kept) + k) * 512, CC, P) for k, n in enumerate(kept)})
        for d in range(2):
            bd[d]["RHS"], bd[d]["U"] = bd[d]["T1"], bd[d]["MT"]
        fin = [at(A_S + k * NTOK, NTOK) for k in range(8)]
        ff = at(A_X + 4096, FC, NTOK)
        ffs = [at(A_X + 4096 + FC * NTOK + k * NTOK, NTOK) for k in range(2)]
        sqf = at(A_X + 4096, 8, NTOK)
        assert A_X + 4096 + (FC + 2) * NTOK <= A_TAIL
        htok = at(A_HTOK, 2, D)
        u = at(A_H, D_FFE)
        Pe, Pw, Pc = at(C_MASK, 2, SLOTS), at(C_MASK + 256, 2, SLOTS), at(C_MASK + 512, 2 * SLOTS)
        rw = at(C_MASK + 768, DC, N_EXP)
        rt = at(C_COS, 2, 96)
        ye = ye_[:, :]
        whi, wlo = ([wparts[:, 2 * k + part, :] for k in range(PARTS)] for part in range(2))
        (hTe, uT), (hTe_lo, uT_lo) = (
            (tparts[:, part, 0:D].rearrange("p (a b) -> p a b", a=DC),
             tparts[:, part, D:D + D_FFE].rearrange("p (a b) -> p a b", a=D_FFE // P)) for part in range(2))
        flat = tparts.rearrange("p a b -> p (a b)")
        h_hi, h_lo = (flat[:, k * DC * NTOK:(k + 1) * DC * NTOK].rearrange("p (a b) -> p a b", a=DC)
                      for k in range(2))
        assert A_TAIL + 2 * PARTS * SLOT2 + 2 * DC * NTOK <= A_RING
        cs_hi, cs_lo = (flat[:, k * 16:(k + 1) * 16].rearrange("p (a b) -> p a b", b=2) for k in range(2))
        sqm = at(A_HTOK, 4, LAT)
        rsm = at(A_HTOK + 1024, 2, LAT)

        loads = []

        def w_src(w, r0, nr, c0, n):
            return w[r0 * P:(r0 + nr) * P, c0:c0 + n].rearrange("(k p) n -> p k n", p=P)

        for l in range(DEPTH):
            for j in range(24):
                loads.append((("ada", l, j), w_src(inp["ada_w"][l], 0, DC, 256 * j, 256), DC, 256))
        proj = [("lora", 3072, 224)]
        for hh, other in enumerate(("aq", "ak")):
            proj += [(f"r{hh}", 1536 + 256 * hh, 256), (f"k{hh}", 2048 + 256 * hh, 256),
                     (f"v{hh}", 2560 + 256 * hh, 256)]
            proj += [(f"{other}{q}", 512 * hh + 256 * q, 256) for q in range(2)]
        proj += [(f"av{hh}", 1024 + 256 * hh, 256) for hh in range(2)]
        for l in range(DEPTH):
            for key, c0, n in proj:
                loads.append(((key, l), w_src(inp["w_in"][l], 0, DC, c0, n), DC, n))
            for j in range(4):
                loads.append((("wout", l, j), w_src(inp["w_out"][l], 0, DC, 256 * j, 256), DC, 256))
            if l == 0:
                for j in range(D_FF // 256):
                    loads.append((("w1", j), w_src(inp["ffn_w1"][0], 0, DC, 256 * j, 256), DC, 256))
                    loads.append((("w3", j), w_src(inp["ffn_w3"][0], 0, DC, 256 * j, 256), DC, 256))
                for j in range(4):
                    for q, (r0, nr) in enumerate([(0, 8), (8, 8), (16, 6)]):
                        loads.append((("w2", j, q), w_src(inp["ffn_w2"][0], r0, nr, 256 * j, 256), nr, 256))
        load_at = {key: n for n, (key, *_) in enumerate(loads)}
        held_back = {load_at["wout", l, 2]: l for l in range(DEPTH)}
        asq = [at(A_RING + (n % RING) * SLOT, CC, NTOK) for n in sorted(held_back)]

        def ring_view(n):
            _, _, nk, nn = loads[n]
            return at(A_RING + (n % RING) * SLOT, nk, nn)

        def ring_wait(pe, key):
            n = load_at[key]
            pe.wait_ge(ring_full[n % RING], 16 * (n // RING + 1))
            return ring_view(n)

        loops = {}
        base = {(e, d): PRIME for e in ("pe", "dve", "act", "pool") for d in range(2)}
        for l in range(DEPTH):
            for s in range(2):
                with_y = s == 1 or l < DEPTH - 1
                lists = loop_lists(with_y, s)
                lc = {}
                for e, lst in zip(("pe", "dve", "act", "pool"), lists):
                    for d in range(2):
                        lc[e, d] = LoopCount(ev(f"chunk_{e}{d}"), base[e, d], lst)
                        base[e, d] = lc[e, d].end(NCH // 2)
                loops[l, s] = (with_y, lc)

        n_small = sum(len(t) for t in VEC_TILES) + 1
        xload_v = 16 * 4

        used_by = {}
        norm_no = {(0, 0): 0, (0, 1): 1, (1, 0): 2, (1, 1): 3, (2, 0): 4}
        w_base = [0, 16]
        LG, MX, R1, R2, CHO, SC, RI, CI, R3, R4, R5 = 0, 8, 16, 24, 32, 40, 48, 59, 70, 78, 86

        fr = range(7)
        def tile_name(m):
            if m < 28:
                return f"W{m}" if m % 2 == 0 else f"{'AB'[(m // 2) % 2]}{m // 4}"
            return f"W{m}" if m < TILES - 1 else "Y1"

        item_banks = ["G0", "G1", "PC"] + sum([[f"A{f}", f"B{f}"] + ([f"T{f - 1}"] if f else []) for f in fr], []) \
            + ["Y0", "Y1", "T6"] + [f"C{g}" for g in range(4)]
        item_pe = ["G0", "G1", "PC"] \
            + sum([[tile_name(4 * f + k) for k in range(4)] + ([f"T{f - 1}"] if f else []) for f in fr], []) \
            + ["W28", "W29", "T6"] + [f"W{m}" for m in range(30, TILES - 1)] + ["Y0", "Y1"] \
            + [f"C{g}" for g in range(4)]
        item_act = ["H0", "H1", "H2", "G0", "G1", "PC"] \
            + sum([[f"H{4 * f + 3}", f"H{4 * f + 4}", f"S{f}", f"H{4 * f + 5}", f"H{4 * f + 6}"]
                   + ([f"T{f - 1}"] if f else []) for f in fr], []) \
            + ["H31", "H32", "T6"] + [f"H{m}" for m in range(33, TILES)] + ["Y0", "Y1"]
        item_dve = ["L0", "G0", "G1", "L1", "L2"] \
            + sum([[f"L{4 * f + 3}", f"L{4 * f + 4}", f"UA{f}", f"L{4 * f + 5}", f"L{4 * f + 6}", f"U{f}"]
                   + ([f"T{f - 1}"] if f else []) for f in fr], []) \
            + ["L31", "L32", "T6"] + [f"L{m}" for m in range(33, TILES)] \
            + ["P0", "P1", "Pw0", "Pw1"] + sum([[f"C{g}a", f"C{g}"] for g in range(4)], [])
        item_cnt = {e: LoopCount(ev(f"item_{e}"), PRIME, lst)
                    for e, lst in (("pe", item_pe), ("act", item_act), ("dve", item_dve))}
        item_reader = {n: ("act", n) for n in ("PC", "Y0", "Y1")}
        item_reader.update({n: ("dve", n) for n in item_banks if n[0] in "GTC"})
        item_reader.update({f"A{f}": ("dve", f"UA{f}") for f in fr})
        item_reader.update({f"B{f}": ("dve", f"U{f}") for f in fr})

        def await_steps(eng, i, needs, earlier=()):
            for e in ("pe", "act", "dve"):
                c_ = item_cnt[e]
                now = [c_.names.index(x) for e_, x in needs if e_ == e]
                past = [c_.names.index(x) for e_, x in earlier if e_ == e]
                if now:
                    eng.wait_ge(c_.sem, c_.after(i, c_.names[max(now)]))
                elif past:
                    eng.wait_ge(c_.sem, c_.in_last(i, c_.names[max(past)]))

        def mu1(l, x_, cc):
            return col[:, K_MU1 + 12 * l + 4 * x_ + cc:K_MU1 + 12 * l + 4 * x_ + cc + 1]

        def x_source(l, n):
            def wait(eng, c):
                if l == 2:
                    eng.wait_ge(ev("items_done"), 1)
                elif n == 1:
                    banks.released(eng, ("wo", l, c))
                else:
                    banks.released(eng, ("xt", c) if l == 0 else ("f2", c))
            return wait

        out_tile = at(A_H, 2, D)
        LAST = stages
        block = ctx.enter_context(nc.Block())

        @block.tensor
        def _(pe):
            mm = nc.tensor.matmul
            for d in range(2):
                pe.sem_inc(ev(f"chunk_pe{d}"), PRIME)
            pe.sem_inc(ev("item_pe"), PRIME)

            def product(key, outs):
                bank = banks.take(pe, key)
                for view, terms in outs:
                    for n, (a, b) in enumerate(terms):
                        ins = mm(view(bank), a, b, start=(n == 0), stop=(n == len(terms) - 1))
                banks.fill(ins, key)
                return ins

            def in_parts(view, a, b, start, stop):
                (a_hi, a_lo), (b_hi, b_lo) = a, b
                mm(view, a_hi, b_hi, start=start, stop=False)
                mm(view, a_lo, b_hi, start=False, stop=False)
                return mm(view, a_hi, b_lo, start=False, stop=stop)

            def setup():
                pe.wait_ge(ev("const_in"), 16)
                pe.wait_ge(ev("vec_in"), 16 * n_small)
                for t, (c0, n) in enumerate(vec_tiles):
                    bank = banks.take(pe, ("vec", t))
                    banks.fill(nc.tensor.transpose(bank[:, 0:n], vec_rows[t][0:n, :], ident[0:n, 0:n]), ("vec", t))
                pe.wait_ge(ev("x_in"), xload_v)
                for c in range(DC):
                    bank = banks.take(pe, ("xt", c))
                    for t in range(4):
                        ins = nc.tensor.transpose(bank[:, t * P:(t + 1) * P], xin[:, t, c * P:(c + 1) * P], ident)
                    banks.fill(ins, ("xt", c))
                pe.wait_ge(ev("cs_parts"), 1)
                for l in range(DEPTH):
                    for j in range(24):
                        t = 24 * l + j
                        pe.wait_ge(ev("ada_lo"), t + 1)
                        hi, lo = (w[t % PARTS].rearrange("p (k n) -> p k n", n=256) for w in (whi, wlo))
                        bank = banks.take(pe, ("ada", l, j))
                        for k in range(DC):
                            ins = in_parts(bank[0:2, 0:256], (cs_hi[:, k, :], cs_lo[:, k, :]),
                                           (hi[:, k, :], lo[:, k, :]), k == 0, k == DC - 1)
                        banks.fill(ins, ("ada", l, j))
                    for j in range(24):
                        banks.released(pe, ("ada", l, j))
                    bank = banks.take(pe, ("mod", l))
                    for j in range(48):
                        ins = nc.tensor.transpose(bank[:, 2 * j:2 * j + 2], modrow[0:2, l, j * P:(j + 1) * P],
                                                  ident[0:2, 0:2])
                    banks.fill(ins, ("mod", l))

            def norm(tag, n0, sqv, w):
                bank = banks.take(pe, ("norm", tag))
                for c in range(DC):
                    pe.wait_ge(ev("norm_sq"), DC * norm_no[tag] + c + 1)
                    ins = mm(bank[:, 0:w], ones, sqv[:, c % 4, 0:w], start=(c == 0), stop=(c == DC - 1))
                    if c < DC - 1:
                        ins.then_inc(ev("norm_used"), 1)
                banks.fill(ins, ("norm", tag))

            def project(l):
                t0 = first(l)

                def by_channel(load, tag, w, q, n, a):
                    bank = banks.take(pe, tag)
                    for k in range(DC):
                        if tag[0] == "wd":
                            pe.wait_ge(ev("h_ready"), DC * norm_no[l, 0] + k + 1)
                        ins = mm(bank[0:n, a:NTOK], w[:, k, q:q + n], hT[:, k, a:NTOK], start=(k == 0),
                                 stop=(k == DC - 1))
                    banks.fill(ins, tag)
                    used_by[load] = tag

                w = ring_wait(pe, ("lora", l))
                by_channel(("lora", l), ("wd", l), w, 0, 64, 0)
                by_channel(("lora", l), ("ad", l), w, 64, 64, 0)
                by_channel(("lora", l), ("gd", l), w, 128, 96, t0)

                def rkv(hh):
                    for nm in "rkv":
                        w = ring_wait(pe, (f"{nm}{hh}", l))
                        for q in range(2):
                            by_channel((f"{nm}{hh}", l), (nm, l, 2 * hh + q), w, q * P, P, t0 if nm == "r" else 0)
                    for q in range(2):
                        pe.wait_ge(ev("kk_sq"), 4 * l + 2 * hh + q + 1)
                        product(("kn", l, 2 * hh + q), [(lambda b: b[:, :], [(onesbd, tA[q])])])

                def rates(cc):
                    banks.released(pe, ("wd", l))
                    banks.released(pe, ("ad", l))
                    pe.wait_ge(ev("lora_w_in"), 48 if l == 0 else 128)
                    for d in range(2):
                        r, cs_ = slice(32 * d, 32 * d + 32), slice(cc * P, (cc + 1) * P)
                        product(("wl", l, cc, d), [(lambda b: b[:, :], [(lw2[r, cs_], th[r, :])])])
                        product(("al", l, cc, d), [(lambda b: b[:, :], [(la2[r, cs_], ad[r, :])])])

                def bonus(cc):
                    pe.wait_ge(ev("bonus_in"), 4 * l + cc + 1)
                    product(("bn", l, cc), [(lambda b: b[:, t0:NTOK], [(onesbd, tA[0][:, t0:NTOK])])])

                def attn(nm, hh, a):
                    w = ring_wait(pe, (f"{nm}{hh}", l))
                    for q in range(2):
                        by_channel((f"{nm}{hh}", l), (nm, l, 2 * hh + q), w, q * P, P, a)

                rkv(0)
                rates(0)
                attn("aq", 0, t0)
                bonus(0)
                rates(1)
                attn("aq", 1, t0)
                bonus(1)
                rkv(1)
                rates(2)
                attn("ak", 0, 0)
                bonus(2)
                rates(3)
                attn("ak", 1, 0)
                bonus(3)
                for hh in range(2):
                    w = ring_wait(pe, (f"av{hh}", l))
                    for t in range(4):
                        product(("vt", l, hh, t), [
                            (lambda b: b[:, 0:256],
                             [(hT[:, k, t * P:(t + 1) * P], w[:, k, :]) for k in range(DC)])])
                    used_by[(f"av{hh}", l)] = ("vt", l, hh, 3)
                if l > 0:
                    for cc in range(CC):
                        banks.released(pe, ("v", l, cc))
                    product(("vv", l), [(lambda b: b[0:32, :], [(lv1[:, k, :], vT[:, k, :]) for k in range(CC)])])
                    banks.released(pe, ("vv", l))
                    for cc in range(CC):
                        product(("vg", l, cc), [(lambda b: b[:, :],
                                                 [(lv2[0:32, cc * P:(cc + 1) * P], th[0:32, :])])])
                for nm, dst in (("aq", qT), ("ak", kT)):
                    for cc in range(CC):
                        banks.released(pe, (nm, l, cc))
                        product(("rope", l, nm, cc), [(lambda b: b[:, 0:LAT], [(perm, dst[:, cc, CTX:NTOK])])])

            def attention(l):
                pe.wait_ge(ev("roped"), 8 * (l + 1))
                for hh in range(2):
                    for t in range(4):
                        banks.released(pe, ("vt", l, hh, t))
                units = [(s, h, qt) for s in streams(l) for h in range(CC) for qt in range(2)]

                def scores(n):
                    s, h, qt = units[n]
                    nk = CTX if s == 0 else NTOK
                    q0 = s * CTX + qt * P
                    for m in range(2):
                        r = slice(64 * m, 64 * m + 64)
                        product(("s", l, n, m), [(lambda b: b[:, 0:nk], [(qT[r, h, q0:q0 + P], kT[r, h, 0:nk])])])

                def turned(n):
                    s, h, qt = units[n]
                    kts = 2 if s == 0 else 4
                    pe.wait_ge(ev("w_ready"), w_base[l] + n + 1)
                    bank = banks.take(pe, ("wt", l, n))
                    for kt in range(kts):
                        ins = nc.tensor.transpose(bank[:, kt * P:(kt + 1) * P], Wm[n % 2][:, kt * P:(kt + 1) * P],
                                                  ident)
                    banks.fill(ins, ("wt", l, n))

                def outputs(n):
                    s, h, qt = units[n]
                    if qt == 1:
                        banks.released(pe, ("wt", l, n - 1))
                        banks.released(pe, ("wt", l, n))
                        product(("o", l, s, h), [(lambda b: b[:, 0:256],
                                                  [(vtok[:, kt, h * P:(h + 1) * P], WT[(n // 2) % 2][:, kt, :])
                                                   for kt in range(2 if s == 0 else 4)])])

                for n in range(len(units) + 3):
                    if n < len(units):
                        scores(n)
                    if n >= 3:
                        outputs(n - 3)
                    if 2 <= n < len(units) + 2:
                        turned(n - 2)
                for h in range(CC):
                    for s in streams(l):
                        banks.released(pe, ("o", l, s, h))
                    t0 = first(l)
                    product(("on", l, h), [(lambda b: b[:, t0:NTOK], [(ones, asq[l][:, h, t0:NTOK])])])

            def chunks(l, s):
                with_y, lc = loops[l, s]
                pl = lc["pe", 0].names
                banks.all_free(pe)

                operands = {
                    "NT": [("B", "Z")], "N": [("Z", "B")], "AZ": [("K", "Z")], "AB": [("B", "R")],
                    "AK": [("K", "R")], "RHS": [("Z", "S"), ("AZ", "VT")], "U": [("XT", "RHS")],
                    "Y": [("S", "R"), ("U", "AB"), ("VT", "AK")], "ST": [("BT", "U"), ("KT", "VT")],
                }
                for b in range(1, LEVELS):
                    operands[f"T{b}"] = [("MT", "X")]
                    operands[f"XT{b}"] = [("T1", "XT")]
                    operands[f"X{b}"] = [("XT", "T1")]
                needs = {
                    "NT": [("pool", "LZ1")], "N": [], "AZ": [], "BT": [], "KT": [], "VT": [],
                    "AB": [("pool", "LR1")] if with_y else [], "AK": [],
                    "RHS": [("dve", "AZ"), ("act", "VT")], "U": [("act", "RHS"), ("act", f"XT{LEVELS - 1}")],
                    "Y": [("act", "U")], "ST": [("act", "U"), ("act", "KT"), ("act", "BT")],
                }
                if with_y:
                    needs["Y"] += [("dve", "AK")]
                for b in range(1, LEVELS):
                    old = [("dve", "Xi"), ("dve", "XTi")] if b == 1 else [("act", f"X{b - 1}"), ("act", f"XT{b - 1}")]
                    needs[f"T{b}"] = [("pool", f"M{b}"), old[0]]
                    needs[f"X{b}"] = [("dve", f"T{b}"), old[1]]
                    needs[f"XT{b}"] = [("dve", f"T{b}"), old[1]]
                reader = {"NT": ("dve", "XTm"), "N": ("dve", "Xm"), "Y": ("dve", "Y1"), "ST": ("dve", "ST1")}
                for nme in pl:
                    if nme not in reader:
                        reader[nme] = ("dve", nme) if nme in lc["dve", 0].names else ("act", nme)
                        assert nme in lc[reader[nme][0], 0].names

                with pe.Fori(0, NCH // 2) as i:
                    for pos, nme in enumerate(pl):
                        for d in range(2):
                            cnt = {e: lc[e, d] for e in ("pe", "dve", "act", "pool")}
                            if pos == 0:
                                pe.wait_ge(cnt["dve"].sem, cnt["dve"].before(i))
                                pe.wait_ge(cnt["act"].sem, cnt["act"].before(i))
                            want = list(needs[nme])
                            if pos >= 4:
                                want.append(reader[pl[pos - 4]])
                            for e in ("pool", "dve", "act"):
                                steps = [step for x_, step in want if x_ == e]
                                if steps:
                                    pe.wait_ge(cnt[e].sem, cnt[e].after(i, max(steps, key=cnt[e].names.index)))
                            bank = psum[4 * d + pos % 4]
                            for cc in range(CC):
                                view = bank[:, cc * P:(cc + 1) * P]
                                if nme in ("BT", "KT", "VT"):
                                    ins = nc.tensor.transpose(view, bd[d][nme[0]][:, cc, :], ident)
                                else:
                                    terms = operands[nme]
                                    for n, (a, b) in enumerate(terms):
                                        ins = mm(view, bd[d][a][:, cc, :], bd[d][b][:, cc, :],
                                                 start=(n == 0), stop=(n == len(terms) - 1))
                            ins.then_inc(cnt["pe"].sem, 1)
                for d in range(2):
                    for e in ("dve", "act"):
                        pe.wait_ge(lc[e, d].sem, lc[e, d].end(NCH // 2))

            def finish(l):
                t0 = first(l)
                for cc in range(CC):
                    product(("ym", l, cc), [(lambda b: b[:, t0:NTOK], [(onesbd, hT[:, 4 + cc, t0:NTOK])])])
                for cc in range(CC):
                    pe.wait_ge(ev("y_sq"), 4 * l + cc + 1)
                    product(("yv", l, cc), [(lambda b: b[:, t0:NTOK], [(onesbd, fin[cc][:, t0:NTOK])])])
                    product(("yg", l, cc), [(lambda b: b[:, t0:NTOK],
                                             [(g2[0:96, cc * P:(cc + 1) * P], sgd[0:96, t0:NTOK])])])

            def w_out(l):
                t0 = first(l)
                for cc in range(CC):
                    banks.released(pe, ("yg", l, cc))
                for j in range(4):
                    w = ring_wait(pe, ("wout", l, j))
                    for q in range(2):
                        product(("wo", l, 2 * j + q), [
                            (lambda b: b[:, t0:NTOK],
                             [(w[:, k, q * P:(q + 1) * P], hT[:, k, t0:NTOK]) for k in range(DC)])])
                    used_by[("wout", l, j)] = ("wo", l, 2 * j + 1)

            def feed_forward():
                for t in range(2 * (D_FF // 256)):
                    nm, j = ("w1", "w3")[t % 2], t // 2
                    pe.wait_ge(ev("ffn_lo"), t + 1)
                    hi, lo = (w[t % PARTS].rearrange("p (k n) -> p k n", n=256) for w in (whi, wlo))
                    for q in range(2):
                        cols_ = slice(q * P, (q + 1) * P)
                        bank = banks.take(pe, (nm, 2 * j + q))
                        for k in range(DC):
                            if t == 0 and q == 0:
                                pe.wait_ge(ev("h_lo"), k + 1)
                            ins = in_parts(bank[:, :], (hi[:, k, cols_], lo[:, k, cols_]),
                                           (h_hi[:, k, :], h_lo[:, k, :]), k == 0, k == DC - 1)
                        banks.fill(ins, (nm, 2 * j + q))
                for j in range(4):
                    pair = [banks.take(pe, ("f2", 2 * j + q)) for q in range(2)]
                    k0 = 0
                    for part, nr in enumerate((8, 8, 6)):
                        w = ring_wait(pe, ("w2", j, part))
                        for q in range(2):
                            for k in range(nr):
                                if j == 0 and q == 0:
                                    banks.released(pe, ("w3", k0 + k))
                                ins = mm(pair[q][:, :], w[:, k, q * P:(q + 1) * P], ff[:, k0 + k, :],
                                         start=(k0 + k == 0), stop=(k0 + k == FC - 1))
                            if part == 2:
                                banks.fill(ins, ("f2", 2 * j + q))
                        if part < 2:
                            ins.then_inc(ev("w2_part"), 1)
                        used_by[("w2", j, part)] = ("f2", 2 * j + 1) if part == 2 else 2 * j + part + 1
                        k0 += nr

            def route():
                pe.wait_ge(ev("h_ready"), DC * (norm_no[1, 1] + 1))
                pe.wait_ge(ev("router_in"), 16)
                for t in range(2):
                    for half in range(2):
                        bank = banks.take(pe, ("ht", t, half))
                        for c in range(4):
                            ins = nc.tensor.transpose(bank[:, c * P:(c + 1) * P],
                                                      hT[:, 4 * half + c, CTX + t * P:CTX + (t + 1) * P], ident)
                        banks.fill(ins, ("ht", t, half))
                for t in range(2):
                    product(("lg", t), [(lambda b: b[:, 0:8], [
                        (hT[:, k, CTX + t * P:CTX + (t + 1) * P], rw[:, k, :]) for k in range(DC)])])
                pe.wait_ge(ev("chosen"), 2)
                ch = [rt[:, t, CHO:CHO + 8] for t in range(2)]
                product(("rk", 0), [(lambda b: b[:, 0:8], [(upper, ch[0])])])
                product(("rk", 1), [(lambda b: b[:, 0:8], [(upper, ch[1]), (ones, ch[0])])])
                product(("ct", 0), [(lambda b: b[:, 0:8], [(ones, ch[0]), (ones, ch[1])])])

            def experts():
                banks.all_free(pe)
                pe.wait_ge(ev("items_ready"), 1)
                T = pe.value_load(idx[0:1, 15:16], min_val=N_EXP, max_val=MAX_ITEMS)
                cnt = item_cnt
                with pe.Fori(0, T) as i:
                    def step(ins):
                        ins.then_inc(cnt["pe"].sem, 1)

                    def begin(nme, needs=(), earlier=()):
                        pos = item_banks.index(nme)
                        needs, earlier = list(needs), list(earlier)
                        if pos >= 8:
                            needs.append(item_reader[item_banks[pos - 8]])
                        else:
                            at_ = max(p_ for p_ in range(len(item_banks)) if p_ % 8 == pos)
                            earlier.append(item_reader[item_banks[at_]])
                        await_steps(pe, i, needs, earlier)
                        return psum[pos % 8]

                    for g in range(2):
                        bank = begin(f"G{g}", earlier=[("dve", "P1")])
                        for c in range(4):
                            for t in range(2):
                                k = 4 * g + c
                                ins = mm(bank[:, c * P:(c + 1) * P], htok[:, t, k * P:(k + 1) * P], Pe[:, t, :],
                                         start=(t == 0), stop=(t == 1))
                        step(ins)
                    bank = begin("PC", earlier=[("dve", "Pw1")])
                    for t in range(2):
                        ins = nc.tensor.transpose(bank[:, t * P:(t + 1) * P], Pw[:, t, :], ident)
                    step(ins)

                    def weights(m, n):
                        return [w[m % PARTS].rearrange("p (k n) -> p k n", n=n) for w in (whi, wlo)]

                    def turn(f):
                        bank = begin(f"T{f}", [("dve", f"U{f}")])
                        for q in range(4):
                            k = 4 * f + q
                            ins = nc.tensor.transpose(bank[:, q * P:(q + 1) * P], u[:, k * P:(k + 1) * P], ident)
                        step(ins)

                    for f in range(7):
                        for x_ in "AB":
                            for half in range(2):
                                m = 4 * f + 2 * (x_ == "B") + half
                                ready = [("dve", f"L{m}"), ("dve", "G1")]
                                if half == 0:
                                    bank = begin(f"{x_}{f}", ready)
                                else:
                                    await_steps(pe, i, ready)
                                hi, lo = weights(m, 512)
                                for q in range(4):
                                    k = 4 * half + q
                                    ins = in_parts(bank[:, :], (hTe[:, k, :], hTe_lo[:, k, :]),
                                                   (hi[:, q, :], lo[:, q, :]), k == 0, k == DC - 1)
                                step(ins)
                        if f:
                            turn(f - 1)
                    for m in range(28, TILES):
                        ready = [("dve", f"L{m}"), ("dve", f"T{(m - 28) // 2}")]
                        if m == 28:
                            b0, b1 = begin("Y0", ready), begin("Y1", ready)
                        else:
                            await_steps(pe, i, ready)
                        hi, lo = weights(m, D)
                        for half, bank in enumerate((b0, b1)):
                            c0 = half * 512
                            for q in range(2):
                                k = 2 * (m - 28) + q
                                ins = in_parts(bank[:, :], (uT[:, k, :], uT_lo[:, k, :]),
                                               (hi[:, q, c0:c0 + 512], lo[:, q, c0:c0 + 512]), k == 0, k == 27)
                            if half == 1 or m == TILES - 1:
                                step(ins)
                        if m == 29:
                            turn(6)
                    for g in range(4):
                        bank = begin(f"C{g}", [("act", f"Y{g // 2}")])
                        for q in range(2):
                            c = 2 * g + q
                            ins = mm(bank[:, q * 256:(q + 1) * 256], ye[:, c * P:(c + 1) * P], Pc, start=True,
                                     stop=True)
                        step(ins)
                pe.wait_ge(ev("items_done"), 1)

            def final():
                for t in range(2):
                    for half in range(2):
                        bank = banks.take(pe, ("fin", t, half))
                        if t == 0 and half == 0:
                            pe.wait_ge(ev("out_scaled"), 1)
                        for c in range(4):
                            ins = nc.tensor.transpose(bank[:, c * P:(c + 1) * P],
                                                      xT[:, 4 * half + c, CTX + t * P:CTX + (t + 1) * P], ident)
                        banks.fill(ins, ("fin", t, half))

            seq = [setup]
            for l in range(DEPTH):
                seq += [lambda l=l: norm((l, 0), 0, sq, NTOK), lambda l=l: project(l), lambda l=l: attention(l),
                        lambda l=l: chunks(l, 0), lambda l=l: chunks(l, 1), lambda l=l: finish(l),
                        lambda l=l: w_out(l)]
                if l == 0:
                    seq += [lambda: norm((0, 1), 0, sqf, NTOK), feed_forward]
                else:
                    seq += [lambda: norm((1, 1), CTX, sqm, LAT), route, experts]
            seq += [lambda: norm((2, 0), CTX, sqm, LAT), final]
            for f in seq[:LAST]:
                f()

        @block.scalar
        def _(act):
            f_ = nc.scalar.activation
            chain = Chain(act, ev("act_chain"))
            for d in range(2):
                act.sem_inc(ev(f"chunk_act{d}"), PRIME)
            act.sem_inc(ev("item_act"), PRIME)

            def copy_out(key, dst, src, scale=1.0, func=ACT.Copy, bias=0.0):
                bank = banks.see(act, key)
                ins = f_(dst, src(bank), func, bias=bias, scale=scale)
                banks.done(ins, key)
                return ins

            def setup():
                act.dma_start(at(A_CONST, N_CONST), inp["const_tables"]).then_inc(ev("const_in"), 16)
                act.dma_start(lamrow.rearrange("p a b c -> p (a b c)"),
                              inp["diff_lambda"].rearrange("l a b -> (l a b)").partition_broadcast(P)
                              ).then_inc(ev("vec_in"), 16)
                for t, tile in enumerate(VEC_TILES):
                    r = 0
                    for name, n in tile:
                        src = inp[name]
                        nd = len(src.shape)
                        flat = {1: "d -> (d)", 2: "a d -> (a d)", 3: "a b d -> (a b d)", 4: "a b e d -> (a b e d)"}
                        src = src.rearrange(flat[nd]) if nd > 1 else src
                        act.dma_start(vec_rows[t][r:r + n, :], src.rearrange("(n p) -> n p", p=P)
                                      ).then_inc(ev("vec_in"), 16)
                        r += n
                for k, src in enumerate((inp["ctx"][0], inp["x"][0])):
                    for t in range(2):
                        act.dma_start(xin[:, 2 * k + t, :], src[t * P:(t + 1) * P, :]).then_inc(ev("x_in"), 16)
                act.wait_ge(ev("vec_cols"), 1)
                f_(col[:, K_SMALL:K_SMALL + 16], vec[:, cols["c"]:cols["c"] + 16], ACT.Sigmoid
                   ).then_inc(ev("c_sig"), 1)
                def high(t):
                    if t >= PARTS:
                        banks.see(act, ("ada", (t - PARTS) // 24, (t - PARTS) % 24))
                    act.wait_ge(ring_full[t % RING], 16 * (t // RING + 1))
                    f_(whi[t % PARTS], at(A_RING + (t % RING) * SLOT, SLOT), ACT.Copy).then_inc(ev("ada_hi"), 1)

                for t in range(PARTS):
                    high(t)
                act.wait_ge(ev("lam_sums"), 1)
                f_(col[:, K_SMALL:K_SMALL + 4], col[:, K_SMALL:K_SMALL + 4], ACT.Exp).then_inc(ev("lam_exp"), 1)
                for l in range(DEPTH):
                    for j in range(24):
                        if 24 * l + j + PARTS < 24 * DEPTH:
                            high(24 * l + j + PARTS)
                        copy_out(("ada", l, j), modrow[0:2, l, j * 256:(j + 1) * 256], lambda b: b[0:2, 0:256])

            def ffn_high(t):
                if t >= 2 * (D_FF // 256):
                    return
                n = load_at[("w1", "w3")[t % 2], t // 2]
                act.wait_ge(ring_full[n % RING], 16 * (n // RING + 1))
                if t >= PARTS:
                    old = t - PARTS
                    banks.see(act, (("w1", "w3")[old % 2], 2 * (old // 2) + 1))
                f_(whi[t % PARTS], at(A_RING + (n % RING) * SLOT, SLOT), ACT.Copy).then_inc(ev("ffn_hi"), 1)

            def norm(tag, c0, sqv, srtv, source):
                no = norm_no[tag]
                w = NTOK - c0
                for c in range(DC):
                    source(act, c)
                    if c >= 4:
                        act.wait_ge(ev("norm_used"), (DC - 1) * no + c - 3)
                    f_(sqv[:, c % 4, 0:w], xT[:, c, c0:NTOK], ACT.Square).then_inc(ev("norm_sq"), 1)
                    if tag == (0, 1) and c >= DC - 1 - PARTS and c < DC - 1:
                        ffn_high(c - (DC - 1 - PARTS))
                bank = banks.see(act, ("norm", tag))
                banks.done(f_(srtv[:, 0:w], bank[:, 0:w], ACT.Sqrt, bias=epsc[NORM_EPS], scale=1.0 / D),
                           ("norm", tag))
                if tag[0] == 2:
                    return
                if tag[1] == 0:
                    act.dma_start(x_dram, xT.rearrange("p a b -> p (a b)")).then_inc(ev("x_parked"), 16)
                l, n = tag
                for c in range(DC):
                    act.wait_ge(ev("h_scaled"), DC * no + c + 1)
                    for s in (streams(l) if n else [0, 1]):
                        r = slice(s * CTX, s * CTX + CTX)
                        ins = f_(hT[:, c, r], hT[:, c, r], ACT.Identity, bias=mod[:, l, 24 * n + c, s:s + 1])
                    ins.then_inc(ev("h_ready"), 1)

            def project(l):
                t0 = first(l)
                if l > 0:
                    act.wait_ge(ev("vf_out"), 16)
                    act.dma_start(vf.rearrange("p a b -> p (a b)"), vf_dram).then_inc(ev("vf_in"), 16)
                copy_out(("wd", l), th[0:64, :], lambda b: b[0:64, :], func=ACT.Tanh)
                copy_out(("ad", l), ad[0:64, :], lambda b: b[0:64, :])
                copy_out(("gd", l), sgd[0:96, t0:NTOK], lambda b: b[0:96, t0:NTOK], func=ACT.Sigmoid)

                def rkv(hh):
                    if hh:
                        act.wait_ge(ev("bonus_in"), 4 * l + 2)
                        banks.see(act, ("bn", l, 1))
                    for x_, nm in enumerate("rkv"):
                        a = t0 if nm == "r" else 0
                        for q in range(2):
                            cc = 2 * hh + q
                            dst = vT[:, cc] if nm == "v" else (rm, km)[x_][:, q]
                            bank = banks.see(act, (nm, l, cc))
                            f_(dst[:, a:NTOK], bank[:, a:NTOK], ACT.Copy, scale=mu1(l, x_, cc)
                               ).then_inc(ev("mix_self"), 1)
                    for q in range(2):
                        cc = 2 * hh + q
                        banks.released(act, ("k", l, cc))
                        chain(f_(kk[:, q], km[:, q], ACT.Copy, scale=vcol("rwkv_k_k", 4 * l + cc)))
                        f_(tA[q], kk[:, q], ACT.Square).then_inc(ev("kk_sq"), 1)
                    for q in range(2):
                        banks.released(act, ("kn", l, 2 * hh + q))
                        f_(tA[q], tA[q], ACT.Sqrt).then_inc(ev("kn_root"), 1)

                def rates(cc):
                    act.wait_ge(ev("kk_ready"), 4 * l + 2 * (cc // 2) + 2)
                    if cc:
                        banks.see(act, ("bn", l, cc - 1))
                    if cc == 0:
                        act.wait_ge(ev("x_parked"), 16 * (l + 1))
                    for d in range(2):
                        no = 8 * l + 2 * cc + d
                        if d:
                            act.wait_ge(ev("rates_used"), no)
                        copy_out(("wl", l, cc, d), tA[0], lambda b: b, func=ACT.Sigmoid,
                                 bias=vcol("rwkv_w0", 8 * l + 4 * d + cc))
                        copy_out(("al", l, cc, d), tA[1], lambda b: b, func=ACT.Sigmoid,
                                 bias=vcol("rwkv_a0", 8 * l + 4 * d + cc))
                        act.wait_ge(ev("sums_ready"), no + 1)
                        incl, excl = (tA[2], tA[3])
                        f_(Ba[d][:, cc], incl, ACT.Exp, scale=DECAY)
                        f_(Ka[d][:, cc], incl, ACT.Exp, scale=DECAY)
                        f_(Ra[d][:, cc], incl, ACT.Exp, scale=-DECAY)
                        f_(wc[:, d, cc, :], wc[:, d, cc, :], ACT.Exp, scale=-DECAY)
                        f_(Za[d][:, cc], excl, ACT.Exp, scale=-DECAY).then_inc(ev("decays"), 1)

                def attn(nm, hh, dst, a):
                    for q in range(2):
                        copy_out((nm, l, 2 * hh + q), dst[:, 2 * hh + q, a:NTOK], lambda b: b[:, a:NTOK])

                rkv(0)
                rates(0)
                attn("aq", 0, qT, t0)
                rates(1)
                attn("aq", 1, qT, t0)
                rkv(1)
                rates(2)
                attn("ak", 0, kT, 0)
                rates(3)
                attn("ak", 1, kT, 0)
                if l == 0:
                    for cc in range(CC):
                        banks.released(act, ("v", l, cc))
                    act.dma_start(vf_dram, vT.rearrange("p a b -> p (a b)")).then_inc(ev("vf_out"), 16)
                for hh in range(2):
                    for t in range(4):
                        copy_out(("vt", l, hh, t), vtok[:, t, hh * 256:(hh + 1) * 256], lambda b: b[:, 0:256])
                if l > 0:
                    copy_out(("vv", l), th[0:32, :], lambda b: b[0:32, :])
                    act.wait_ge(ev("rates_used"), 8 * (l + 1))
                    banks.see(act, ("bn", l, 3))
                    for cc in range(CC):
                        copy_out(("vg", l, cc), tA[cc], lambda b: b, func=ACT.Sigmoid, bias=vcol("rwkv_v0", cc))

            def attention(l):
                units = [(s, h, qt) for s in streams(l) for h in range(CC) for qt in range(2)]
                for n in range(len(units) + 3):
                    if n < len(units):
                        nk = CTX if units[n][0] == 0 else NTOK
                        act.wait_ge(ev("max_ready"), w_base[l] + n + 1)
                        for m in range(2):
                            if n >= 2:
                                act.wait_ge(ev("w_ready"), w_base[l] + n - 1)
                            bank = banks.see(act, ("s", l, n, m))
                            banks.done(f_(Pm[n % 2][m][:, 0:nk], bank[:, 0:nk], ACT.Exp,
                                          bias=stat[:, n % 2, 2 + m:3 + m], scale=QK ** -0.5,
                                          accum_out=stat[:, n % 2, 4 + m:5 + m]), ("s", l, n, m))
                    if n >= 3 and units[n - 3][2] == 1:
                        s, h, qt = units[n - 3]
                        r = slice(s * CTX, (s + 1) * CTX)
                        bank = banks.see(act, ("o", l, s, h))
                        f_(hT[:, h, r], bank[:, 0:256], ACT.Copy)
                        banks.done(f_(asq[l][:, h, r], bank[:, 0:256], ACT.Square), ("o", l, s, h))
                    if 2 <= n < len(units) + 2:
                        s, h, qt = units[n - 2]
                        kts = 2 if s == 0 else 4
                        copy_out(("wt", l, n - 2), WT[((n - 2) // 2) % 2][:, 0:kts, qt * P:(qt + 1) * P],
                                 lambda b: b[:, 0:kts * P].rearrange("p (a b) -> p a b", a=kts))
                t0 = first(l)
                for h in range(CC):
                    copy_out(("on", l, h), asq[l][:, h, t0:NTOK], lambda b: b[:, t0:NTOK], func=ACT.Sqrt,
                             bias=epsc[SUBLN_EPS], scale=1.0 / P)

            def chunks(l, s):
                with_y, lc = loops[l, s]
                with act.Fori(0, NCH // 2) as i:
                    for nme in lc["act", 0].names:
                        for d in range(2):
                            pe_c, own = lc["pe", d], lc["act", d]
                            act.wait_ge(pe_c.sem, pe_c.after(i, nme))
                            bank = psum[4 * d + pe_c.names.index(nme) % 4]
                            dst = bd[d][nme.rstrip("12345") if nme[0] == "X" else nme]
                            f_(dst.rearrange("p a b -> p (a b)"), bank, ACT.Copy).then_inc(own.sem, 1)

            def finish(l):
                t0 = first(l)
                for d in range(2):
                    c_ = loops[l, 1][1]["pe", d]
                    act.wait_ge(c_.sem, c_.end(NCH // 2))
                    g_ = loops[l, 1][1]["pool", d]
                    act.wait_ge(g_.sem, g_.end(NCH // 2))
                act.dma_start(xT.rearrange("p a b -> p (a b)"), x_dram).then_inc(ev("x_back"), 16)
                for cc in range(CC):
                    banks.released(act, ("ym", l, cc))
                    f_(fin[cc][:, t0:NTOK], hT[:, 4 + cc, t0:NTOK], ACT.Square).then_inc(ev("y_sq"), 1)
                for cc in range(CC):
                    copy_out(("yv", l, cc), fin[cc][:, t0:NTOK], lambda b: b[:, t0:NTOK], func=ACT.Sqrt,
                             bias=epsc[LNX_EPS], scale=1.0 / CH)

            def feed_forward():
                for j in range(FC // 2):
                    for c in (2 * j, 2 * j + 1):
                        bank = banks.see(act, ("w1", c))
                        if c >= 2:
                            banks.released(act, ("w1", c - 2))
                        f_(ffs[c % 2], bank, ACT.Sigmoid).then_inc(ev("ff_sig"), 1)
                    ffn_high(2 * j + 3)
                    ffn_high(2 * j + 4)

            def route():
                for t in range(2):
                    for half in range(2):
                        copy_out(("ht", t, half), htok[:, t, half * 512:(half + 1) * 512], lambda b: b)
                act.wait_ge(ev("gate_in"), 1)
                for t in range(2):
                    ins = f_(rt[:, t, SC + 1:SC + 2], rt[:, t, SC:SC + 1], ACT.Exp)
                ins.then_inc(ev("gate_exp"), 1)

            def experts():
                act.wait_ge(ev("items_ready"), 1)
                T = act.value_load(idx[0:1, 15:16], min_val=N_EXP, max_val=MAX_ITEMS)
                cnt = item_cnt
                with act.Fori(0, T) as i:
                    for nme in item_act:
                        k = int(nme[1:]) if nme != "PC" else 0
                        if nme[0] == "H":
                            act.wait_ge(ev(f"ring2_full{k % RING2}"), i * (16 * TILES // RING2) + 16 * (k // RING2 + 1))
                            old = ("pe", tile_name((k - PARTS) % TILES))
                            await_steps(act, i, [old] if k >= PARTS else [], [old] if k < PARTS else [])
                            f_(whi[k % PARTS], at(A_RING2 + (k % RING2) * SLOT2, SLOT2), ACT.Copy
                               ).then_inc(cnt["act"].sem, 1)
                            continue
                        made = f"A{k}" if nme[0] == "S" else nme
                        await_steps(act, i, [("pe", made)])
                        src = psum[item_banks.index(made) % 8]
                        fn = ACT.Copy
                        if nme[0] == "G":
                            dst = hTe[:, 4 * k:4 * k + 4, :].rearrange("p a b -> p (a b)")
                        elif nme == "PC":
                            dst, src = Pc, src[:, 0:256]
                        elif nme[0] == "S":
                            dst, fn = u[:, k * 512:(k + 1) * 512], ACT.Sigmoid
                        elif nme[0] == "T":
                            dst = uT[:, 4 * k:4 * k + 4, :].rearrange("p a b -> p (a b)")
                        else:
                            dst = ye[:, k * 512:(k + 1) * 512]
                        f_(dst, src, fn).then_inc(cnt["act"].sem, 1)

            seq = [setup]
            for l in range(DEPTH):
                seq += [lambda l=l: norm((l, 0), 0, sq, srt, x_source(l, 0)), lambda l=l: project(l),
                        lambda l=l: attention(l), lambda l=l: chunks(l, 0), lambda l=l: chunks(l, 1),
                        lambda l=l: finish(l), lambda: None]
                if l == 0:
                    seq += [lambda: norm((0, 1), 0, sqf, sqf[:, 4], x_source(0, 1)), feed_forward]
                else:
                    seq += [lambda: norm((1, 1), CTX, sqm, rsm[:, 0], x_source(1, 1)), route, experts]
            seq += [lambda: norm((2, 0), CTX, sqm, rsm[:, 0], x_source(2, 0)), lambda: None]
            for f in seq[:LAST]:
                f()

        @block.vector
        def _(dve):
            v = nc.vector
            chain = Chain(dve, ev("dve_chain"))
            for d in range(2):
                dve.sem_inc(ev(f"chunk_dve{d}"), PRIME)
            dve.sem_inc(ev("item_dve"), PRIME)

            def setup():
                for k, eps in enumerate((NORM_EPS, SUBLN_EPS, LNX_EPS)):
                    chain(v.memset(col[:, K_EPS + k:K_EPS + k + 1], eps))
                for t, (c0, n) in enumerate(vec_tiles):
                    bank = banks.see(dve, ("vec", t))
                    banks.done(v.tensor_copy(vec[:, c0:c0 + n], bank[:, 0:n]), ("vec", t))
                for t in range(3):
                    banks.released(dve, ("vec", t))
                chain(v.memset(col[:, K_SMALL + 15:K_SMALL + 16], 0.0))
                dve.sem_inc(ev("vec_cols"), 1)
                dve.wait_ge(ev("c_sig"), 1)
                cvec, csig = vec[:, cols["c"]:cols["c"] + 16], col[:, K_SMALL:K_SMALL + 16]
                chain(v.tensor_tensor(cs[:, :, 1], cvec[:, 0:8], csig[:, 0:8], ALU.mult))
                v.tensor_tensor(cs[:, :, 0], cvec[:, 8:16], csig[:, 8:16], ALU.mult).then_inc(ev("cs_ready"), 1)
                dve.wait_ge(ev("cs_ready"), 1)
                chain(v.tensor_copy(cs_hi, cs))
                v.tensor_tensor(cs_lo, cs, cs_hi, ALU.subtract).then_inc(ev("cs_parts"), 1)
                for c in range(DC):
                    bank = banks.see(dve, ("xt", c))
                    banks.done(v.tensor_copy(xT[:, c, :], bank), ("xt", c))

                def low(t):
                    dve.wait_ge(ev("ada_hi"), t + 1)
                    v.tensor_tensor(wlo[t % PARTS], at(A_RING + (t % RING) * SLOT, SLOT), whi[t % PARTS],
                                    ALU.subtract).then_inc(ev("ada_lo"), 1)

                for t in range(PARTS):
                    low(t)
                for l in range(DEPTH):
                    for k in range(2):
                        chain(v.tensor_tensor_reduce(lamtmp, lamrow[:, l, 2 * k, :], lamrow[:, l, 2 * k + 1, :], 1.0,
                                                     0.0, ALU.mult, ALU.add,
                                                     col[:, K_SMALL + 2 * l + k:K_SMALL + 2 * l + k + 1]))
                dve.sem_inc(ev("lam_sums"), 1)
                for t in range(PARTS, 2 * PARTS):
                    low(t)
                dve.wait_ge(ev("lam_exp"), 1)
                for l in range(DEPTH):
                    lam_init = 0.8 - 0.6 * math.exp(-0.3 * l)
                    e = col[:, K_SMALL + 2 * l:K_SMALL + 2 * l + 2]
                    chain(v.tensor_tensor(col[:, K_LAM + l:K_LAM + l + 1], e[:, 0:1], e[:, 1:2], ALU.subtract))
                    chain(v.tensor_scalar(col[:, K_NLAM + l:K_NLAM + l + 1], col[:, K_LAM + l:K_LAM + l + 1],
                                          lam_init, -1.0, ALU.add, ALU.mult))
                    chain(v.tensor_scalar(col[:, K_SUBG + l:K_SUBG + l + 1], vcol("subln_g", l), 1.0 - lam_init, None,
                                          ALU.mult))
                    for x_ in range(3):
                        c0 = K_MU1 + 12 * l + 4 * x_
                        m0 = cols["rwkv_mu"] + (l * 3 + x_) * 8
                        chain(v.tensor_tensor(col[:, c0:c0 + 4], vec[:, m0:m0 + 4], vec[:, m0 + 4:m0 + 8], ALU.add))
                        chain(v.tensor_scalar(col[:, c0:c0 + 4], col[:, c0:c0 + 4], -1.0, 1.0, ALU.mult, ALU.add))
                    chain(v.tensor_scalar(col[:, K_KA1 + 4 * l:K_KA1 + 4 * l + 4],
                                          vec[:, cols["rwkv_k_a"] + 4 * l:cols["rwkv_k_a"] + 4 * l + 4], -1.0, 1.0,
                                          ALU.mult, ALU.add))
                dve.sem_inc(ev("cols_ready"), 1)
                for l in range(DEPTH):
                    for t in range(max(2 * PARTS, 24 * l + PARTS), min(24 * (l + 1) + PARTS, 24 * DEPTH)):
                        low(t)
                    bank = banks.see(dve, ("mod", l))
                    c0 = cols["ada_b"] + 48 * l
                    banks.done(v.tensor_tensor(mod[:, l, :, :], bank[:, 0:96].rearrange("p (a b) -> p a b", b=2),
                                               vec[:, c0:c0 + 48].unsqueeze(2).broadcast_to([P, 48, 2]), ALU.add),
                               ("mod", l))
                    banks.released(dve, ("mod", l))
                    for n in range(2):
                        c0 = cols[f"norm{n + 1}_g"] + 8 * l
                        chain(v.scalar_tensor_tensor(
                            gain[:, 2 * l + n, :, :], mod[:, l, 24 * n + 8:24 * n + 16, :], 1.0,
                            vec[:, c0:c0 + 8].unsqueeze(2).broadcast_to([P, 8, 2]), ALU.add, ALU.mult))

            def ffn_low(t):
                if t >= 2 * (D_FF // 256):
                    return
                n = load_at[("w1", "w3")[t % 2], t // 2]
                dve.wait_ge(ev("ffn_hi"), t + 1)
                v.tensor_tensor(wlo[t % PARTS], at(A_RING + (n % RING) * SLOT, SLOT), whi[t % PARTS],
                                ALU.subtract).then_inc(ev("ffn_lo"), 1)

            def norm(tag, c0, srtv, rstv):
                w = NTOK - c0
                if tag == (0, 1):
                    for t in range(PARTS):
                        ffn_low(t)
                banks.released(dve, ("norm", tag))
                chain(v.reciprocal(rstv[:, 0:w], srtv[:, 0:w]))
                l, n = tag
                for c in range(DC):
                    if l == 2:
                        ins = v.scalar_tensor_tensor(xT[:, c, c0:NTOK], xT[:, c, c0:NTOK], vcol("final_g", c),
                                                     rstv[:, 0:w], ALU.mult, ALU.mult)
                        continue
                    for s in (streams(l) if n else [0, 1]):
                        r = slice(s * CTX, (s + 1) * CTX)
                        ro = slice(s * CTX - c0, (s + 1) * CTX - c0)
                        ins = v.scalar_tensor_tensor(hT[:, c, r], xT[:, c, r], gain[:, 2 * l + n, c, s:s + 1],
                                                     rstv[:, ro], ALU.mult, ALU.mult)
                    ins.then_inc(ev("h_scaled"), 1)
                if l == 2:
                    ins.then_inc(ev("out_scaled"), 1)

            def project(l):
                t0 = first(l)

                def mix(nm, x_, cc, q, no):
                    dst = vT[:, cc] if nm == "v" else (rm, km)[x_][:, q]
                    bank = banks.see(dve, (nm, l, cc))
                    ss = streams(l) if nm == "r" else [0, 1]
                    a, n = ss[0] * CTX, len(ss)
                    dv_ = dst[:, a:NTOK].rearrange("p (s t) -> p s t", s=n)
                    pv = bank[:, a:NTOK].rearrange("p (s t) -> p s t", s=n)
                    m0 = (l * 3 + x_) * 8 + cc
                    dve.wait_ge(ev("mix_self"), no)
                    chain(v.scalar_tensor_tensor(dv_[:, :, 1:CTX], pv[:, :, 0:CTX - 1], vcol("rwkv_mu", m0),
                                                 dv_[:, :, 1:CTX], ALU.mult, ALU.add))
                    banks.done(v.scalar_tensor_tensor(dv_[:, :, 0:CTX - 1], pv[:, :, 1:CTX],
                                                      vcol("rwkv_mu", m0 + 4), dv_[:, :, 0:CTX - 1], ALU.mult,
                                                      ALU.add), (nm, l, cc))

                def rkv(hh):
                    no = 12 * l + 6 * hh
                    for x_, nm in enumerate("rkv"):
                        for q in range(2):
                            no += 1
                            mix(nm, x_, 2 * hh + q, q, no)
                    for q in range(2):
                        bank = banks.see(dve, ("kn", l, 2 * hh + q))
                        banks.done(v.tensor_scalar(tA[q], bank, 1e-24, None, ALU.max), ("kn", l, 2 * hh + q))
                    for q in range(2):
                        cc = 2 * hh + q
                        dve.wait_ge(ev("kn_root"), 4 * l + cc + 1)
                        chain(v.reciprocal(tA[q], tA[q]))
                        v.tensor_tensor(kk[:, q], kk[:, q], tA[q], ALU.mult).then_inc(ev("kk_ready"), 1)
                    dve.wait_ge(ev("kk_ready"), 4 * l + 2 * hh + 2)

                def rates(cc):
                    q = cc % 2
                    for nm in "rkv":
                        banks.released(dve, (nm, l, cc))
                    for d in range(2):
                        no = 8 * l + 2 * cc + d
                        banks.released(dve, ("wl", l, cc, d))
                        banks.released(dve, ("al", l, cc, d))
                        chain(v.tensor_tensor_scan(tA[2], reset, tA[0], 0.0, ALU.mult, ALU.add))
                        chain(v.tensor_tensor(tA[3], tA[2], tA[0], ALU.subtract))
                        by = lambda t: t.rearrange("p (c t) -> p c t", c=NCH)
                        ends = by(tA[2])[:, :, CH - 1]
                        chain(v.tensor_copy(wc[:, d, cc, :], ends))
                        if d == 1:
                            tot = wc[:, d, cc, :].unsqueeze(2).broadcast_to([P, NCH, CH])
                            chain(v.tensor_tensor(by(tA[0]), tot, by(tA[3]), ALU.subtract))
                            chain(v.tensor_tensor(by(tA[3]), tot, by(tA[2]), ALU.subtract))
                            chain(v.tensor_copy(tA[2], tA[0]))
                        dve.sem_inc(ev("sums_ready"), 1)
                        chain(v.tensor_tensor(tA[0], kk[:, q], tA[1], ALU.mult))
                        chain(v.tensor_scalar(tA[1], tA[1], vcol("rwkv_k_a", 4 * l + cc),
                                              col[:, K_KA1 + 4 * l + cc:K_KA1 + 4 * l + cc + 1], ALU.mult, ALU.add))
                        chain(v.tensor_tensor(tA[1], tA[1], km[:, q], ALU.mult))
                        if d == 0:
                            chain(v.tensor_copy(tA[4], tA[1]))
                        else:
                            chain(v.tensor_tensor(tA[4], tA[4], tA[1], ALU.add))
                        dve.wait_ge(ev("decays"), no + 1)
                        v.tensor_tensor(Ba[d][:, cc], Ba[d][:, cc], tA[0], ALU.mult)
                        v.tensor_tensor(Ka[d][:, cc], Ka[d][:, cc], tA[1], ALU.mult)
                        v.scalar_tensor_tensor(Za[d][:, cc], Za[d][:, cc], -1.0, kk[:, q], ALU.mult, ALU.mult)
                        v.tensor_tensor(Ra[d][:, cc, t0:NTOK], Ra[d][:, cc, t0:NTOK], rm[:, q, t0:NTOK], ALU.mult
                                        ).then_inc(ev("rates_used"), 1)
                        dve.wait_ge(ev("rates_used"), no + 1)
                    v.scalar_tensor_tensor(tA[0][:, t0:NTOK], tA[4][:, t0:NTOK], vcol("rwkv_r_k", 4 * l + cc),
                                           rm[:, q, t0:NTOK], ALU.mult, ALU.mult).then_inc(ev("bonus_in"), 1)

                def bonus(cc):
                    bank = banks.see(dve, ("bn", l, cc))
                    banks.done(v.tensor_copy(bon[:, cc, t0:NTOK], bank[:, t0:NTOK]), ("bn", l, cc))

                chain(v.memset(reset, 1.0))
                chain(v.memset(reset.rearrange("p (c t) -> p c t", c=NCH)[:, :, 0:1], 0.0))
                for hh in range(2):
                    rkv(hh)
                    for q in range(2):
                        rates(2 * hh + q)
                        bonus(2 * hh + q)
                if l > 0:
                    dve.wait_ge(ev("vf_in"), 16)
                    for cc in range(CC):
                        banks.released(dve, ("vg", l, cc))
                        chain(v.tensor_tensor(vf[:, cc], vf[:, cc], vT[:, cc], ALU.subtract))
                        chain(v.tensor_tensor(vf[:, cc], vf[:, cc], tA[cc], ALU.mult))
                        chain(v.tensor_tensor(vT[:, cc], vT[:, cc], vf[:, cc], ALU.add))
                for cc in range(CC):
                    banks.released(dve, ("bn", l, cc))
                    chain(v.tensor_tensor(bon[:, cc, t0:NTOK], bon[:, cc, t0:NTOK], vT[:, cc, t0:NTOK], ALU.mult))
                rot = rm[:, 0, 0:LAT]
                for nm, dst in (("aq", qT), ("ak", kT)):
                    for cc in range(CC):
                        bank = banks.see(dve, ("rope", l, nm, cc))
                        banks.done(v.tensor_tensor(rot, bank[:, 0:LAT], sin, ALU.mult), ("rope", l, nm, cc))
                        banks.released(dve, ("rope", l, nm, cc))
                        z = dst[:, cc, CTX:NTOK]
                        chain(v.tensor_tensor(z, z, cos, ALU.mult))
                        chain(v.tensor_tensor(z, z, rot, ALU.add))
                        dve.sem_inc(ev("roped"), 1)

            def attention(l):
                units = [(s, h, qt) for s in streams(l) for h in range(CC) for qt in range(2)]

                def maxima(n):
                    nk = CTX if units[n][0] == 0 else NTOK
                    st = stat[:, n % 2, :]
                    for m in range(2):
                        bank = banks.see(dve, ("s", l, n, m))
                        chain(v.reduce_max(st[:, m:m + 1], bank[:, 0:nk], AX.X))
                    v.tensor_scalar(st[:, 2:4], st[:, 0:2], -(QK ** -0.5), None, ALU.mult
                                    ).then_inc(ev("max_ready"), 1)

                def weights(n):
                    nk = CTX if units[n][0] == 0 else NTOK
                    st = stat[:, n % 2, :]
                    for m in range(2):
                        banks.released(dve, ("s", l, n, m))
                    chain(v.reciprocal(st[:, 6:8], st[:, 4:6]))
                    chain(v.tensor_tensor(st[:, 7:8], st[:, 7:8], col[:, K_NLAM + l:K_NLAM + l + 1], ALU.mult))
                    if n >= 2:
                        banks.see(dve, ("wt", l, n - 2))
                    w = Wm[n % 2][:, 0:nk]
                    chain(v.tensor_scalar(w, Pm[n % 2][0][:, 0:nk], st[:, 6:7], None, ALU.mult))
                    v.scalar_tensor_tensor(w, Pm[n % 2][1][:, 0:nk], st[:, 7:8], w, ALU.mult, ALU.add
                                           ).then_inc(ev("w_ready"), 1)

                for n in range(len(units) + 1):
                    if n < len(units):
                        maxima(n)
                    if n > 0:
                        weights(n - 1)

            def chunks(l, s):
                with_y, lc = loops[l, s]
                idb = ident.unsqueeze(1).broadcast_to([P, CC, P])
                t0 = first(l)
                dve.wait_ge(ev("cleared"), l + 1)
                if s == 0:
                    for h in range(CC):
                        banks.released(dve, ("on", l, h))
                left = dve.alloc_register(f"left_dve{l}{s}")
                dve.reg_mov(left, NCH // 2 - 1)
                with dve.Fori(0, NCH // 2) as i:
                    back = dve.snap(left, min_val=0, max_val=NCH // 2 - 1)
                    for nme in lc["dve", 0].names:
                        for d in range(2):
                            t, own, pe_c = bd[d], lc["dve", d], lc["pe", d]
                            chunk = (i if d == 0 else back) + 4 * s

                            def bank(product):
                                dve.wait_ge(pe_c.sem, pe_c.after(i, product))
                                b = psum[4 * d + pe_c.names.index(product) % 4]
                                return b.rearrange("p (a b) -> p a b", a=CC)
                            if nme == "NTs":
                                ins = v.tensor_tensor(t["NT"], bank("NT"), mask(d, 0), ALU.mult)
                            elif nme == "XTm":
                                ins = v.tensor_tensor(t["XT"], bank("NT"), mask(d, 2), ALU.mult)
                            elif nme == "Xm":
                                ins = v.tensor_tensor(t["X"], bank("N"), mask(1 - d, 2), ALU.mult)
                            elif nme in ("XTi", "Xi"):
                                dve.wait_ge(own.sem, own.after(i, nme[:-1] + "m"))
                                z = t[nme[:-1]]
                                ins = v.tensor_tensor(z, z, idb, ALU.add)
                            elif nme == "AZ":
                                ins = v.tensor_tensor(t["AZ"], bank("AZ"), mask(d, 0), ALU.mult)
                            elif nme in ("AB", "AK"):
                                ins = v.tensor_tensor(t[nme], bank(nme), mask(d, 1), ALU.mult)
                            elif nme[0] == "T":
                                ins = v.tensor_tensor(t["T1"], bank(nme), idb, ALU.add)
                            elif nme == "AN":
                                root = asq[l][:, bass.ds(i, 1), t0:NTOK]
                                if d == 0:
                                    ins = v.reciprocal(root, root)
                                else:
                                    dve.wait_ge(lc["dve", 0].sem, lc["dve", 0].after(i, "AN"))
                                    z = hT[:, bass.ds(i, 1), t0:NTOK]
                                    ins = v.scalar_tensor_tensor(z, z, col[:, K_SUBG + l:K_SUBG + l + 1], root,
                                                                 ALU.mult, ALU.mult)
                            elif nme[0] == "Y":
                                h = int(nme[1])
                                r = slice(64 * h, 64 * h + 64)
                                y = hT[r, 4:8, bass.ds(chunk * CH, CH)]
                                ins = v.tensor_tensor(y, y, bank("Y")[r, :, 64 * h:64 * h + 64], ALU.add)
                            elif nme == "ST1":
                                ins = v.tensor_tensor(t["S"], t["S"], bank("ST"), ALU.add)
                            elif nme == "ST2":
                                dve.wait_ge(own.sem, own.after(i, "ST1"))
                                w = wc[:, d, :, bass.ds(chunk, 1)].broadcast_to([P, CC, P])
                                ins = v.tensor_tensor(t["S"], t["S"], w, ALU.mult)
                            ins.then_inc(own.sem, 1)
                    dve.reg_sub(left, left, 1)

            def finish(l):
                t0 = first(l)
                for cc in range(CC):
                    z = hT[:, 4 + cc, t0:NTOK]
                    bank = banks.see(dve, ("ym", l, cc))
                    banks.done(v.scalar_tensor_tensor(z, bank[:, t0:NTOK], -1.0 / CH, z, ALU.mult, ALU.add),
                               ("ym", l, cc))
                for cc in range(CC):
                    z = hT[:, 4 + cc, t0:NTOK]
                    banks.released(dve, ("yv", l, cc))
                    inv = fin[cc][:, t0:NTOK]
                    chain(v.reciprocal(inv, inv))
                    chain(v.scalar_tensor_tensor(z, z, vcol("lnx_w", 4 * l + cc), inv, ALU.mult, ALU.mult))
                    chain(v.scalar_tensor_tensor(z, z, vcol("lnx_b", 4 * l + cc), bon[:, cc, t0:NTOK], ALU.add,
                                                 ALU.add))
                    bank = banks.see(dve, ("yg", l, cc))
                    banks.done(v.tensor_tensor(z, z, bank[:, t0:NTOK], ALU.mult), ("yg", l, cc))

            def add_gated(keys, l, g):
                for c in range(DC):
                    bank = banks.see(dve, keys(c))
                    for s in streams(l):
                        r = slice(s * CTX, (s + 1) * CTX)
                        ins = v.scalar_tensor_tensor(xT[:, c, r], bank[:, r], mod[:, l, g + c, s:s + 1], xT[:, c, r],
                                                     ALU.mult, ALU.add)
                    banks.done(ins, keys(c))

            def w_out(l):
                dve.wait_ge(ev("x_back"), 16 * (l + 1))
                add_gated(lambda c: ("wo", l, c), l, 16)

            def feed_forward():
                for c in range(DC):
                    dve.wait_ge(ev("h_hi"), c + 1)
                    v.tensor_tensor(h_lo[:, c, :], hT[:, c, :], h_hi[:, c, :], ALU.subtract
                                    ).then_inc(ev("h_lo"), 1)
                for j in range(FC // 2):
                    for c in (2 * j, 2 * j + 1):
                        bank = banks.see(dve, ("w1", c))
                        dve.wait_ge(ev("ff_sig"), c + 1)
                        banks.done(v.tensor_tensor(ff[:, c, :], ffs[c % 2], bank, ALU.mult), ("w1", c))
                    ffn_low(2 * j + 3)
                    for c in (2 * j, 2 * j + 1):
                        bank = banks.see(dve, ("w3", c))
                        banks.released(dve, ("w1", c))
                        banks.done(v.tensor_tensor(ff[:, c, :], ff[:, c, :], bank, ALU.mult), ("w3", c))
                    ffn_low(2 * j + 4)
                add_gated(lambda c: ("f2", c), 0, 40)

            def route():
                big = 1000.0

                def w8(t, k, n=8):
                    return rt[:, t, k:k + n]

                for t in range(2):
                    bank = banks.see(dve, ("lg", t))
                    banks.done(v.tensor_copy(w8(t, LG), bank[:, 0:8]), ("lg", t))
                    banks.released(dve, ("lg", t))
                for t in range(2):
                    chain(v.max(w8(t, MX), w8(t, LG)))
                    chain(v.memset(w8(t, R5), 1.0))
                    chain(v.tensor_scalar(w8(t, R1), w8(t, LG), w8(t, MX, 1), None, ALU.is_equal))
                    chain(v.tensor_tensor_scan(w8(t, R2), w8(t, R5), w8(t, R1), 0.0, ALU.mult, ALU.add))
                    chain(v.scalar_tensor_tensor(w8(t, R1), w8(t, R2), 1.0, w8(t, R1), ALU.is_equal, ALU.mult))
                    chain(v.tensor_scalar(w8(t, R4), w8(t, R1), -1.0, 1.0, ALU.mult, ALU.add))
                    chain(v.scalar_tensor_tensor(w8(t, R3), w8(t, LG), w8(t, MX + 1, 1), w8(t, R4), ALU.is_equal,
                                                 ALU.mult))
                    chain(v.tensor_tensor_scan(w8(t, R2), w8(t, R5), w8(t, R3), 0.0, ALU.mult, ALU.add))
                    chain(v.scalar_tensor_tensor(w8(t, R3), w8(t, R2), 1.0, w8(t, R3), ALU.is_equal, ALU.mult))
                    chain(v.tensor_tensor(w8(t, CHO), w8(t, R1), w8(t, R3), ALU.add))
                    dve.sem_inc(ev("chosen"), 1)
                    chain(v.tensor_tensor(w8(t, SC, 1), w8(t, MX + 1, 1), w8(t, MX, 1), ALU.subtract))
                dve.sem_inc(ev("gate_in"), 1)
                dve.wait_ge(ev("gate_exp"), 1)
                for t in range(2):
                    chain(v.tensor_scalar(w8(t, SC + 2, 1), w8(t, SC + 1, 1), 1.0, None, ALU.add))
                    chain(v.reciprocal(w8(t, SC + 3, 1), w8(t, SC + 2, 1)))
                    chain(v.tensor_tensor(w8(t, SC + 4, 1), w8(t, SC + 1, 1), w8(t, SC + 3, 1), ALU.mult))
                    chain(v.tensor_scalar(w8(t, R3), w8(t, R3), w8(t, SC + 4, 1), None, ALU.mult))
                    chain(v.scalar_tensor_tensor(w8(t, CI), w8(t, R1), w8(t, SC + 3, 1), w8(t, R3), ALU.mult,
                                                 ALU.add))
                    bank = banks.see(dve, ("rk", t))
                    chain(v.scalar_tensor_tensor(w8(t, RI), bank[:, 0:8], big, w8(t, CHO), ALU.add, ALU.mult))
                    banks.done(v.tensor_scalar(w8(t, RI), w8(t, RI), -big, None, ALU.add), ("rk", t))
                    banks.released(dve, ("rk", t))
                bank = banks.see(dve, ("ct", 0))
                t1, t2, t3, t4, one = w8(0, R1), w8(0, R2), w8(0, R3), w8(0, R4), w8(0, R5)
                banks.done(v.tensor_scalar(t1, bank[:, 0:8], float(SLOTS), None, ALU.is_gt), ("ct", 0))
                banks.released(dve, ("ct", 0))
                chain(v.tensor_tensor_scan(t2, one, t1, 0.0, ALU.mult, ALU.add))
                ids = w8(1, R1, 16)
                chain(v.memset(ids, 0.0))
                chain(v.tensor_copy(ids[:, 0:8], iota[:, 0:8]))
                chain(v.tensor_scalar(ids[:, 15:16], t2[:, 7:8], float(N_EXP), None, ALU.add))
                for r in range(MAX_ITEMS - N_EXP):
                    chain(v.scalar_tensor_tensor(t3, t2, float(r + 1), t1, ALU.is_equal, ALU.mult))
                    chain(v.tensor_tensor_reduce(t4, t3, iota[:, 0:8], 1.0, 0.0, ALU.mult, ALU.add,
                                                 ids[:, 8 + r:9 + r]))
                    for t in range(2):
                        z = w8(t, RI + 8 + r, 1)
                        chain(v.tensor_scalar(w8(1, R4), w8(t, RI), 2 * big - SLOTS, None, ALU.add))
                        chain(v.tensor_tensor_reduce(t4, t3, w8(1, R4), 1.0, 0.0, ALU.mult, ALU.add, z))
                        chain(v.tensor_scalar(z, z, -2 * big, None, ALU.add))
                        chain(v.tensor_tensor_reduce(t4, t3, w8(t, CI), 1.0, 0.0, ALU.mult, ALU.add,
                                                     w8(t, CI + 8 + r, 1)))
                chain(v.tensor_copy(idx[:, :], ids))
                for t in range(2):
                    chain(choose(t, 0))
                for t in range(2):
                    chain(choose_weighted(t, 0))
                dve.sem_inc(ev("items_ready"), 1)

            def choose(t, i):
                return v.tensor_scalar(Pe[:, t, :], iota, rt[:, t, bass.ds(i + RI, 1)], None, ALU.is_equal)

            def choose_weighted(t, i):
                return v.tensor_scalar(Pw[:, t, :], iota, rt[:, t, bass.ds(i + RI, 1)],
                                       rt[:, t, bass.ds(i + CI, 1)], ALU.is_equal, ALU.mult)

            def experts():
                T = dve.value_load(idx[0:1, 15:16], min_val=N_EXP, max_val=MAX_ITEMS)
                own = item_cnt["dve"]
                with dve.Fori(0, T) as i:
                    for nme in item_dve:
                        if nme[0] == "L":
                            m = int(nme[1:])
                            await_steps(dve, i, [("act", f"H{m}")])
                            ins = v.tensor_tensor(wlo[m % PARTS], at(A_RING2 + (m % RING2) * SLOT2, SLOT2),
                                                  whi[m % PARTS], ALU.subtract)
                        elif nme[0] in "GT":
                            k = int(nme[1:])
                            await_steps(dve, i, [("act", nme)])
                            hi, lo = (hTe, hTe_lo) if nme[0] == "G" else (uT, uT_lo)
                            part = lambda z: z[:, 4 * k:4 * k + 4, :].rearrange("p a b -> p (a b)")
                            ins = v.tensor_tensor(part(lo), psum[item_banks.index(nme) % 8], part(hi), ALU.subtract)
                        elif nme[0] == "U":
                            f = int(nme[-1])
                            z = u[:, f * 512:(f + 1) * 512]
                            if nme[1] == "A":
                                await_steps(dve, i, [("act", f"S{f}")])
                                bank = psum[item_banks.index(f"A{f}") % 8]
                            else:
                                await_steps(dve, i, [("dve", f"UA{f}"), ("pe", f"B{f}")])
                                bank = psum[item_banks.index(f"B{f}") % 8]
                            ins = v.tensor_tensor(z, z, bank, ALU.mult)
                        elif nme[0] == "P":
                            await_steps(dve, i, [("pe", "PC")])
                            ins = (choose_weighted if nme[1] == "w" else choose)(int(nme[-1]), i + 1)
                        else:
                            g = int(nme[1])
                            await_steps(dve, i, [("pe", f"C{g}")])
                            q = 0 if nme[-1] == "a" else 1
                            c = 2 * g + q
                            z = xT[:, c, CTX:NTOK]
                            ins = v.scalar_tensor_tensor(z, psum[item_banks.index(f"C{g}") % 8][:, q * 256:(q + 1) * 256],
                                                         mod[:, 1, 40 + c, 1:2], z, ALU.mult, ALU.add)
                        ins.then_inc(own.sem, 1)
                dve.wait_ge(own.sem, T * own.per + own.base)
                dve.sem_inc(ev("items_done"), 1)

            def final():
                for t in range(2):
                    for half in range(2):
                        bank = banks.see(dve, ("fin", t, half))
                        banks.done(v.tensor_copy(out_tile[:, t, half * 512:(half + 1) * 512], bank),
                                   ("fin", t, half))

            seq = [setup]
            for l in range(DEPTH):
                seq += [lambda l=l: norm((l, 0), 0, srt, rst), lambda l=l: project(l), lambda l=l: attention(l),
                        lambda l=l: chunks(l, 0), lambda l=l: chunks(l, 1), lambda l=l: finish(l),
                        lambda l=l: w_out(l)]
                if l == 0:
                    seq += [lambda: norm((0, 1), 0, sqf[:, 4], sqf[:, 5]), feed_forward]
                else:
                    seq += [lambda: norm((1, 1), CTX, rsm[:, 0], rsm[:, 1]), route, experts]
            seq += [lambda: norm((2, 0), CTX, rsm[:, 0], rsm[:, 1]), final]
            for f in seq[:LAST]:
                f()

        @block.gpsimd
        def _(pool):
            g = nc.gpsimd
            chain = Chain(pool, ev("pool_chain"))
            for d in range(2):
                pool.sem_inc(ev(f"chunk_pool{d}"), PRIME)

            def chunks(l, s):
                with_y, lc = loops[l, s]
                if s == 0:
                    pool.wait_ge(ev("roped"), 8 * (l + 1))
                    chain(g.memset(at(A_KEPT, 2 * len(kept) * 512), 0.0))
                    chain(g.memset(hT[:, 4:8, first(l):NTOK], 0.0))
                    pool.sem_inc(ev("cleared"), 1)
                last_use = {"B": "AB" if with_y else "BT", "K": "AK" if with_y else "KT", "V": "VT", "Z": "RHS"}
                if with_y:
                    last_use["R"] = "Y"
                now, past = lc["pe", 0], loops[l, 0][1]["pe", 0]
                past_use = dict(last_use) if past.names == now.names else {"B": "BT", "K": "KT", "V": "VT", "Z": "RHS"}
                for a, x in past_use.items():
                    k = max(now.names.index(last_use[a]), now.per - past.per + past.names.index(x))
                    last_use[a] = now.names[k]
                arrays = {"Z": Za, "R": Ra, "B": Ba, "K": Ka, "V": [vT, vT]}
                left = pool.alloc_register(f"left_pool{l}{s}")
                pool.reg_mov(left, NCH // 2 - 1)
                with pool.Fori(0, NCH // 2) as i:
                    back = pool.snap(left, min_val=0, max_val=NCH // 2 - 1)
                    for nme in lc["pool", 0].names:
                        for d in range(2):
                            t, own, pe_c, dve_c = bd[d], lc["pool", d], lc["pe", d], lc["dve", d]
                            if (nme, d) == (own.names[0], 0):
                                pool.wait_ge(lc["pool", 1].sem, lc["pool", 1].before(i))
                            elif d == 0:
                                pool.wait_ge(lc["pool", 1].sem, lc["pool", 1].after(i, before))
                            else:
                                pool.wait_ge(lc["pool", 0].sem, lc["pool", 0].after(i, nme))
                            if nme[0] == "L":
                                a, h = nme[1], int(nme[2])
                                pool.wait_ge(pe_c.sem, pe_c.in_last(i, last_use[a]))
                                tok = ((i if d == 0 else back) + 4 * s) * CH
                                r = slice(64 * h, 64 * h + 64)
                                ins = g.tensor_copy(t[a][r, :, 64 * h:64 * h + 64],
                                                    arrays[a][d][r, :, bass.ds(tok, CH)])
                            else:
                                b = int(nme[1:])
                                pool.wait_ge(dve_c.sem, dve_c.after(i, "NTs"))
                                if b > 1:
                                    pool.wait_ge(pe_c.sem, pe_c.after(i, f"T{b - 1}"))
                                ins = g.tensor_tensor(t["MT"], t["NT"], mask(d, 2 + b), ALU.mult)
                            ins.then_inc(own.sem, 1)
                        before = nme
                    pool.reg_sub(left, left, 1)

            def feed_forward():
                for c in range(DC):
                    pool.wait_ge(ev("h_ready"), DC * norm_no[0, 1] + c + 1)
                    g.tensor_copy(h_hi[:, c, :], hT[:, c, :]).then_inc(ev("h_hi"), 1)
                    pool.wait_ge(ev("h_hi"), c + 1)

            nop = lambda: None
            seq = [nop]
            for l in range(DEPTH):
                seq += [nop, nop, nop, lambda l=l: chunks(l, 0), lambda l=l: chunks(l, 1), nop, nop]
                seq += [nop, feed_forward] if l == 0 else [nop, nop, nop]
            for f in seq[:LAST]:
                f()

        @block.sync
        def _(sp):
            def ring_load(n):
                key, src, nk, nn = loads[n]
                if n >= RING:
                    old = loads[n - RING][0]
                    if old[0] == "ada":
                        sp.wait_ge(ev("ada_lo"), n - RING + 1)
                    elif old[0] in ("w1", "w3"):
                        sp.wait_ge(ev("ffn_lo"), 2 * old[1] + (old[0] == "w3") + 1)
                    else:
                        free_slot(sp, used_by[old])
                if n in held_back:
                    c_ = loops[held_back[n], 0][1]["dve", 1]
                    sp.wait_ge(c_.sem, c_.end(NCH // 2))
                sp.dma_start(ring_view(n), src).then_inc(ring_full[n % RING], 16)

            def free_slot(eng, use):
                if isinstance(use, tuple):
                    banks.see(eng, use)
                else:
                    eng.wait_ge(ev("w2_part"), use)

            done = [0]

            def load_until(key):
                n = load_at[key]
                while done[0] <= n:
                    ring_load(done[0])
                    done[0] += 1

            def setup():
                load_until(("ada", DEPTH - 1, 23))

            def project(l):
                if l == 0:
                    banks.see(sp, ("mod", DEPTH - 1))
                else:
                    banks.see(sp, ("yg", 0, CC - 1))
                    for d in range(2):
                        c_ = loops[0, 1][1]["pe", d]
                        sp.wait_ge(c_.sem, c_.end(NCH // 2))
                ws = [(lw2[0:64, :], inp["rwkv_w2"][l].rearrange("a j n -> (a j) n")),
                      (la2[0:64, :], inp["rwkv_a2"][l].rearrange("a j n -> (a j) n")),
                      (g2[0:96, :], inp["rwkv_g2"][l])]
                if l:
                    ws += [(lv1, inp["rwkv_v1"][0].rearrange("(k p) n -> p k n", p=P)),
                           (lv2[0:32, :], inp["rwkv_v2"][0])]
                for dst, src in ws:
                    sp.dma_start(dst, src).then_inc(ev("lora_w_in"), 16)
                load_until(("av1", l))

            def w_out(l):
                load_until(("wout", l, 3))

            def feed_forward():
                load_until(("w2", 3, 2))

            def route():
                banks.released(sp, ("yg", 1, CC - 1))
                sp.wait_ge(ev("h_ready"), DC * (norm_no[1, 1] + 1))
                sp.dma_start(rw, inp["router_w"][0].rearrange("(k p) n -> p k n", p=P)
                             ).then_inc(ev("router_in"), 16)

            def expert_load(m, e):
                dst = at(A_RING2 + (m % RING2) * SLOT2, SLOT2)
                if m < 28:
                    w = inp["exp_w1" if (m // 2) % 2 == 0 else "exp_w3"]
                    f, half = m // 4, m % 2
                    src = w[0, bass.ds(e, 1), half * 512:(half + 1) * 512, f * 512:(f + 1) * 512]
                    dst = dst.rearrange("p (k n) -> p k n", n=512)
                else:
                    src = inp["exp_w2"][0, bass.ds(e, 1), (m - 28) * 256:(m - 27) * 256, :]
                    dst = dst.rearrange("p (k n) -> p k n", n=D)
                sp.dma_start(dst, src.rearrange("e (k p) n -> p (e k) n", p=P)
                             ).then_inc(ev(f"ring2_full{m % RING2}"), 16)

            def experts():
                sp.wait_ge(ev("items_ready"), 1)
                T = sp.value_load(idx[0:1, 15:16], min_val=N_EXP, max_val=MAX_ITEMS)
                own = item_cnt["dve"]
                with sp.Fori(0, T) as i:
                    e = sp.value_load(idx[0:1, bass.ds(i, 1)], min_val=0, max_val=N_EXP - 1)
                    for m in range(TILES):
                        old = ("dve", f"L{(m - RING2) % TILES}")
                        await_steps(sp, i, [old] if m >= RING2 else [], [old] if m < RING2 else [])
                        expert_load(m, e)

            def final():
                for t in range(2):
                    for half in range(2):
                        banks.released(sp, ("fin", t, half))
                    sp.dma_start(out[0, t * P:(t + 1) * P, :], out_tile[:, t, :]).then_inc(ev("out_written"), 16)
                sp.wait_ge(ev("out_written"), 32)

            nop = lambda: None
            seq = [setup]
            for l in range(DEPTH):
                seq += [nop, lambda l=l: project(l), nop, nop, nop, nop, lambda l=l: w_out(l)]
                seq += [nop, feed_forward] if l == 0 else [nop, route, experts]
            seq += [nop, final]
            for f in seq[:LAST]:
                f()
            if LAST > 1:
                sp.wait_ge(ev("x_parked"), 16 * (2 if LAST > 10 else 1))
            if LAST > 2:
                sp.wait_ge(ev("vf_out"), 16)


_INS = ["x", "c", "ctx", "c_ctx", "ada_w", "ada_b", "norm1_g", "norm2_g", "w_in", "w_out", "diff_lambda", "subln_g",
        "rwkv_mu", "rwkv_w0", "rwkv_w2", "rwkv_a0", "rwkv_a2", "rwkv_v0", "rwkv_v1", "rwkv_v2", "rwkv_g2",
        "rwkv_k_k", "rwkv_k_a", "rwkv_r_k", "lnx_w", "lnx_b", "ffn_w1", "ffn_w3", "ffn_w2", "router_w", "exp_w1",
        "exp_w3", "exp_w2", "final_g"]


def kernel(**inputs):
    import concourse.bacc as _bacc
    from concourse.bass_utils import run_bass_kernel_spmd as _run

    nc = _bacc.Bacc("TRN2", target_bir_lowering=False, num_devices=1)
    arrays, aps = {}, {}
    for name in _INS:
        a = np.ascontiguousarray(inputs[name])
        arrays[f"in_{name}"] = a
        aps[name] = nc.dram_tensor(f"in_{name}", a.shape, mybir.dt.from_np(a.dtype), kind="ExternalInput").ap()
    tables = constant_tables()
    arrays["in_const_tables"] = tables
    aps["const_tables"] = nc.dram_tensor("in_const_tables", tables.shape, F32, kind="ExternalInput").ap()
    out = nc.dram_tensor("out_0", (1, LAT, D), F32, kind="ExternalOutput").ap()
    vf_dram = nc.dram_tensor("first_values", (P, CC * NTOK), F32).ap()
    x_dram = nc.dram_tensor("parked_x", (P, DC * NTOK), F32).ap()
    hybrid_backbone(nc, aps, out, vf_dram, x_dram)
    r = _run(nc, [arrays], core_ids=[0])
    return r.results[0]["out_0"]
```
